# Optimizing a Trainium2 kernel written in Bass

```python
import jax, jax.numpy as jnp
from jax import lax
import numpy as np
import math

D_MODEL = 1024
BATCH = 1
SEQ = 256
DEPTH = 1

CHUNK = 64
N_HEADS = 8
HEAD_DIM = 64
ATTN_WIDTH = N_HEADS * HEAD_DIM
N_IDX_HEADS = 4
IDX_DIM = 64
TOPK_MAX = 256
Q_BLOCK = 128
POOL_WINDOWS = (2, 4, 8, 16)
N_POOL_GROUPS = 4
POOL_WIDTH = 512
POOL_GROUP = POOL_WIDTH // N_POOL_GROUPS
N_BRANCHES = 2
PEER_HEADS = 8
PEER_QDIM = 128
PEER_HALF = PEER_QDIM // 2
N_KEYS = 128
N_EXPERTS = N_KEYS * N_KEYS
PEER_TOPK = 16
TOKEN_BLOCK = 128
EPS = 1e-6
IN_SIZES = (ATTN_WIDTH, HEAD_DIM, HEAD_DIM, N_IDX_HEADS * IDX_DIM, IDX_DIM, N_IDX_HEADS, POOL_WIDTH, N_BRANCHES * D_MODEL)
IN_WIDTH = sum(IN_SIZES)


def rms_norm(x, g):
    x32 = x.astype(jnp.float32)
    y = x32 * lax.rsqrt(jnp.mean(x32 * x32, axis=-1, keepdims=True) + EPS)
    return (y * g.astype(jnp.float32)).astype(x.dtype)

def dsa_attention(q, k, v, iq, ik, iw):
    B, S = q.shape[0], q.shape[1]
    n_sel = min(TOPK_MAX, S // 4)
    n_blk = S // Q_BLOCK
    key_chunk = jnp.arange(S) // CHUNK
    idx_scale = IDX_DIM ** -0.5
    w_scale = N_IDX_HEADS ** -0.5
    attn_scale = HEAD_DIM ** -0.5

    def to_blocks(a):
        return jnp.swapaxes(a.reshape((B, n_blk, Q_BLOCK) + a.shape[2:]), 0, 1)

    def gather_rows(table, idx):
        return jax.vmap(lambda tb, ib: tb[ib])(table, idx)

    def one_block(args):
        qb, iqb, iwb, blk = args
        q_chunk = (blk * Q_BLOCK + jnp.arange(Q_BLOCK)) // CHUNK
        admissible = key_chunk[None, :] <= q_chunk[:, None]
        rel = jax.nn.relu(jnp.einsum('bqhd,bsd->bqhs', iqb, ik) * idx_scale)
        score = jnp.einsum('bqhs,bqh->bqs', rel, iwb * w_scale).astype(jnp.float32)
        score = jnp.where(admissible[None], score, -jnp.inf)
        _, sel = lax.top_k(score, n_sel)
        k_sel = gather_rows(k, sel)
        v_sel = gather_rows(v, sel)
        ok = key_chunk[sel] <= q_chunk[None, :, None]
        logits = jnp.einsum('bqhd,bqkd->bqhk', qb, k_sel).astype(jnp.float32) * attn_scale
        logits = jnp.where(ok[:, :, None, :], logits, -jnp.inf)
        p = jax.nn.softmax(logits, axis=-1).astype(v.dtype)
        return jnp.einsum('bqhk,bqkd->bqhd', p, v_sel)

    out = lax.map(one_block, (to_blocks(q), to_blocks(iq), to_blocks(iw), jnp.arange(n_blk)))
    return jnp.swapaxes(out, 0, 1).reshape(B, S, ATTN_WIDTH)

def pool_mixer(p, w_grp, s_pool):
    B, S = p.shape[0], p.shape[1]
    pg = p.reshape(B, S, N_POOL_GROUPS, POOL_GROUP).astype(jnp.float32)
    cs = jnp.pad(jnp.cumsum(pg, axis=1), ((0, 0), (1, 0), (0, 0), (0, 0)))
    t = jnp.arange(S)
    outs = []
    for g, w in enumerate(POOL_WINDOWS):
        cs_g = cs[:, :, g, :]
        lo = jnp.maximum(t + 1 - w, 0)
        cnt = (t + 1 - lo).astype(jnp.float32)
        mean = (cs_g[:, t + 1] - cs_g[:, lo]) / cnt[None, :, None]
        outs.append(mean - pg[:, :, g, :])
    mixed = jnp.stack(outs, axis=2).astype(p.dtype)
    mixed = jnp.einsum('bsgc,gcd->bsgd', mixed, w_grp) * s_pool
    return mixed.reshape(B, S, POOL_WIDTH)

def peer_ffn(h, w_q, sub_keys, u, v):
    B, S, D = h.shape
    n_blk = (B * S) // TOKEN_BLOCK
    hb = h.reshape(n_blk, TOKEN_BLOCK, D)

    def one_block(hx):
        q = (hx @ w_q).reshape(TOKEN_BLOCK, PEER_HEADS, 2, PEER_HALF)
        s = jnp.einsum('nhpd,hpkd->nhpk', q, sub_keys).astype(jnp.float32)
        top_s, top_i = lax.top_k(s, PEER_TOPK)
        cand = top_s[:, :, 0, :, None] + top_s[:, :, 1, None, :]
        best_s, best_p = lax.top_k(cand.reshape(TOKEN_BLOCK, PEER_HEADS, PEER_TOPK * PEER_TOPK), PEER_TOPK)
        i1 = jnp.take_along_axis(top_i[:, :, 0], best_p // PEER_TOPK, axis=-1)
        i2 = jnp.take_along_axis(top_i[:, :, 1], best_p % PEER_TOPK, axis=-1)
        expert = (i1 * N_KEYS + i2).reshape(TOKEN_BLOCK, PEER_HEADS * PEER_TOPK)
        gate = jax.nn.softmax(best_s, axis=-1).reshape(TOKEN_BLOCK, PEER_HEADS * PEER_TOPK).astype(hx.dtype)
        u_sel = u[expert]
        v_sel = v[expert]
        act = jax.nn.gelu(jnp.einsum('nd,ned->ne', hx, u_sel), approximate=False)
        return jnp.einsum('ne,ned->nd', gate * act, v_sel)

    return lax.map(one_block, hb).reshape(B, S, D)

def first_inputs(seed: int = 0) -> dict:
    key = jax.random.key(seed)
    ks = jax.random.split(key, 20)
    f32 = jnp.float32
    D = D_MODEL

    def nrm(k, shape, scale):
        return jax.random.normal(k, shape, f32) * scale

    return {
        'x': nrm(ks[0], (BATCH, SEQ, D), 1.0),
        'c': nrm(ks[1], (BATCH, D), 1.0),
        'w_ada': nrm(ks[2], (DEPTH, D, 6 * D), 0.5 * D ** -0.5),
        'b_ada': nrm(ks[3], (DEPTH, 6 * D), 0.02),
        'g_norm1': 1.0 + nrm(ks[4], (DEPTH, D), 0.02),
        'w_in': nrm(ks[5], (DEPTH, D, IN_WIDTH), D ** -0.5),
        'g_q': 1.0 + nrm(ks[6], (DEPTH, HEAD_DIM), 0.02),
        'g_k': 1.0 + nrm(ks[7], (DEPTH, HEAD_DIM), 0.02),
        'g_ik': 1.0 + nrm(ks[8], (DEPTH, IDX_DIM), 0.02),
        'w_pool_grp': nrm(ks[9], (DEPTH, N_POOL_GROUPS, POOL_GROUP, POOL_GROUP), POOL_GROUP ** -0.5),
        's_pool': 1.0 + nrm(ks[10], (DEPTH, N_POOL_GROUPS, POOL_GROUP), 0.1),
        'w_up_attn': nrm(ks[11], (DEPTH, ATTN_WIDTH, D), ATTN_WIDTH ** -0.5),
        'w_up_pool': nrm(ks[12], (DEPTH, POOL_WIDTH, D), POOL_WIDTH ** -0.5),
        'w_out': nrm(ks[13], (DEPTH, D, D), D ** -0.5),
        'g_norm2': 1.0 + nrm(ks[14], (DEPTH, D), 0.02),
        'w_peer_q': nrm(ks[15], (DEPTH, D, PEER_HEADS * PEER_QDIM), D ** -0.5),
        'peer_subkeys': nrm(ks[16], (DEPTH, PEER_HEADS, 2, N_KEYS, PEER_HALF), PEER_HALF ** -0.5),
        'peer_u': nrm(ks[17], (DEPTH, N_EXPERTS, D), D ** -0.5),
        'peer_v': nrm(ks[18], (DEPTH, N_EXPERTS, D), 0.5),
    }

def first_block(x, c, w_ada, b_ada, g_norm1, w_in, g_q, g_k, g_ik, w_pool_grp, s_pool,
              w_up_attn, w_up_pool, w_out, g_norm2, w_peer_q, peer_subkeys, peer_u, peer_v):
    B, S, D = x.shape
    cuts = [int(v) for v in np.cumsum(IN_SIZES)[:-1]]
    for layer in range(DEPTH):
        ada = c @ w_ada[layer] + b_ada[layer]
        shift1, scale1, gate1, shift2, scale2, gate2 = [a[:, None, :] for a in jnp.split(ada, 6, axis=-1)]

        h = rms_norm(x, g_norm1[layer]) * (1.0 + scale1) + shift1
        z = h @ w_in[layer]
        zq, zk, zv, ziq, zik, ziw, zp, zg = jnp.split(z, cuts, axis=-1)
        q = rms_norm(zq.reshape(B, S, N_HEADS, HEAD_DIM), g_q[layer])
        k = rms_norm(zk, g_k[layer])
        iq = ziq.reshape(B, S, N_IDX_HEADS, IDX_DIM)
        ik = rms_norm(zik, g_ik[layer])
        y_attn = dsa_attention(q, k, zv, iq, ik, ziw) @ w_up_attn[layer]
        y_pool = pool_mixer(zp, w_pool_grp[layer], s_pool[layer]) @ w_up_pool[layer]
        g_attn, g_pool = jnp.split(jax.nn.sigmoid(zg), 2, axis=-1)
        mixed = (g_attn * y_attn + g_pool * y_pool) @ w_out[layer]
        x = x + gate1 * mixed

        h2 = rms_norm(x, g_norm2[layer]) * (1.0 + scale2) + shift2
        x = x + gate2 * peer_ffn(h2, w_peer_q[layer], peer_subkeys[layer], peer_u[layer], peer_v[layer])
    return x


DEPTH_2 = 2

N_MIXERS = 2
N_A = (DEPTH_2 + 1) // N_MIXERS
N_B = DEPTH_2 // N_MIXERS

S5_WIDTH = D_MODEL
S5_GROUP = 16
S5_GROUPS = S5_WIDTH // S5_GROUP
S5_STATE = 64
S5_CHUNK = 128
S5_DT_MIN = 1e-3
S5_DT_MAX = 1e-1

HEAD_DIM_2 = D_MODEL // N_HEADS
ATTN_WIDTH_2 = N_HEADS * HEAD_DIM_2
MOBA_BLOCK = 256
MOBA_TOPK = 3
ROPE_THETA = 500000.0
ROT_DIM = HEAD_DIM_2 // 4

D_FF = 2816
MACARON_WEIGHT = 0.5


def rms_norm_2(x, g):
    xf = x.astype(jnp.float32)
    y = xf * lax.rsqrt(jnp.mean(xf * xf, axis=-1, keepdims=True) + EPS)
    return (y * g.astype(jnp.float32)).astype(x.dtype)

def swiglu(h, w_gate, w_up, w_down):
    return (jax.nn.silu(h @ w_gate) * (h @ w_up)) @ w_down

def cmul(ar, ai, br, bi):
    return ar * br - ai * bi, ar * bi + ai * br

def s5_mixer(h, w_in, a_re, a_im, log_dt, b_re, b_im, c_re, c_im, d_skip, w_glu, w_out):
    f32 = jnp.float32
    bsz, seq, _ = h.shape
    u = (h @ w_in).astype(f32)
    dt = jnp.exp(log_dt.astype(f32))[:, None]
    a_re = a_re.astype(f32)
    a_im = a_im.astype(f32)
    mag = jnp.exp(a_re * dt)
    lam_re = mag * jnp.cos(a_im * dt)
    lam_im = mag * jnp.sin(a_im * dt)
    den = a_re * a_re + a_im * a_im
    num_re = lam_re - 1.0
    coef_re = (num_re * a_re + lam_im * a_im) / den
    coef_im = (lam_im * a_re - num_re * a_im) / den
    bb_re, bb_im = cmul(coef_re[..., None], coef_im[..., None], b_re.astype(f32), b_im.astype(f32))
    c_re = c_re.astype(f32)
    c_im = c_im.astype(f32)
    n_chunks = seq // S5_CHUNK
    u_chunks = u.reshape(bsz, n_chunks, S5_CHUNK, S5_GROUPS, S5_GROUP).transpose(1, 0, 2, 3, 4)
    lam_re_b = jnp.broadcast_to(lam_re, (bsz, S5_CHUNK, S5_GROUPS, S5_STATE))
    lam_im_b = jnp.broadcast_to(lam_im, (bsz, S5_CHUNK, S5_GROUPS, S5_STATE))

    def combine(left, right):
        a1r, a1i, b1r, b1i = left
        a2r, a2i, b2r, b2i = right
        ar, ai = cmul(a2r, a2i, a1r, a1i)
        br, bi = cmul(a2r, a2i, b1r, b1i)
        return ar, ai, br + b2r, bi + b2i

    def step(carry, u_c):
        h_re0, h_im0 = carry
        bu_re = jnp.einsum('bcgn,gpn->bcgp', u_c, bb_re)
        bu_im = jnp.einsum('bcgn,gpn->bcgp', u_c, bb_im)
        pr, pi, sr, si = lax.associative_scan(combine, (lam_re_b, lam_im_b, bu_re, bu_im), axis=1)
        cr, ci = cmul(pr, pi, h_re0[:, None], h_im0[:, None])
        st_re = sr + cr
        st_im = si + ci
        y = jnp.einsum('bcgp,gnp->bcgn', st_re, c_re) - jnp.einsum('bcgp,gnp->bcgn', st_im, c_im)
        return (st_re[:, -1], st_im[:, -1]), y

    init = (jnp.zeros((bsz, S5_GROUPS, S5_STATE), f32), jnp.zeros((bsz, S5_GROUPS, S5_STATE), f32))
    _, ys = lax.scan(step, init, u_chunks)
    y = ys.transpose(1, 0, 2, 3, 4).reshape(bsz, seq, S5_WIDTH) + d_skip.astype(f32) * u
    g = jax.nn.gelu(y)
    g = g * jax.nn.sigmoid(g @ w_glu.astype(f32))
    return g.astype(h.dtype) @ w_out

def partial_rope(x, cos, sin):
    half = ROT_DIM // 2
    x1 = x[..., :half]
    x2 = x[..., half:ROT_DIM]
    c = cos[None, :, None, :]
    s = sin[None, :, None, :]
    return jnp.concatenate([x1 * c - x2 * s, x2 * c + x1 * s, x[..., ROT_DIM:]], axis=-1)

def moba_mixer(h, w_qkv, q_gain, k_gain, w_out):
    f32 = jnp.float32
    bsz, seq, _ = h.shape
    qkv = (h @ w_qkv).reshape(bsz, seq, 3, N_HEADS, HEAD_DIM_2)
    q = rms_norm_2(qkv[:, :, 0], q_gain).astype(f32)
    k = rms_norm_2(qkv[:, :, 1], k_gain).astype(f32)
    v = qkv[:, :, 2].astype(f32)
    pos = jnp.arange(seq, dtype=f32)
    inv_freq = ROPE_THETA ** (-jnp.arange(0, ROT_DIM, 2, dtype=f32) / ROT_DIM)
    ang = pos[:, None] * inv_freq[None, :]
    cos, sin = jnp.cos(ang), jnp.sin(ang)
    q = partial_rope(q, cos, sin) * (HEAD_DIM_2 ** -0.5)
    k = partial_rope(k, cos, sin)
    n_blocks = -(-seq // MOBA_BLOCK)
    pad = n_blocks * MOBA_BLOCK - seq
    k_pad = jnp.pad(k, ((0, 0), (0, pad), (0, 0), (0, 0)))
    v_pad = jnp.pad(v, ((0, 0), (0, pad), (0, 0), (0, 0)))
    k_blk = k_pad.reshape(bsz, n_blocks, MOBA_BLOCK, N_HEADS, HEAD_DIM_2)
    v_blk = v_pad.reshape(bsz, n_blocks, MOBA_BLOCK, N_HEADS, HEAD_DIM_2)
    k_mean = k_blk.mean(axis=2)
    k_bh = k_blk.transpose(0, 3, 1, 2, 4)
    v_bh = v_blk.transpose(0, 3, 1, 2, 4)
    top_k = min(MOBA_TOPK, n_blocks)
    b_idx = jnp.arange(bsz)[:, None, None]
    h_idx = jnp.arange(N_HEADS)[None, None, :]
    blk_ids = jnp.arange(n_blocks)

    def attend_chunk(c):
        start = c * Q_BLOCK
        q_c = lax.dynamic_slice_in_dim(q, start, Q_BLOCK, axis=1)
        q_pos = start + jnp.arange(Q_BLOCK)
        own = start // MOBA_BLOCK
        gate = jnp.einsum('bqhd,bnhd->bqhn', q_c, k_mean)
        gate = jnp.where(blk_ids < own, gate, -jnp.inf)
        _, sel = lax.top_k(gate, top_k)
        k_own = lax.dynamic_slice_in_dim(k_pad, own * MOBA_BLOCK, MOBA_BLOCK, axis=1)
        v_own = lax.dynamic_slice_in_dim(v_pad, own * MOBA_BLOCK, MOBA_BLOCK, axis=1)
        k_pos = own * MOBA_BLOCK + jnp.arange(MOBA_BLOCK)
        s_own = jnp.einsum('bqhd,bkhd->bqhk', q_c, k_own)
        causal = (k_pos[None, :] <= q_pos[:, None])[None, :, None, :]
        s_own = jnp.where(causal, s_own, -jnp.inf)
        scores = []
        for j in range(top_k):
            k_sel = k_bh[b_idx, h_idx, sel[..., j]]
            s_j = jnp.einsum('bqhd,bqhkd->bqhk', q_c, k_sel)
            scores.append(jnp.where(j < own, s_j, -jnp.inf))
        scores.append(s_own)
        p = jax.nn.softmax(jnp.concatenate(scores, axis=-1), axis=-1)
        p_parts = jnp.split(p, top_k + 1, axis=-1)
        out = jnp.einsum('bqhk,bkhd->bqhd', p_parts[-1], v_own)
        for j in range(top_k):
            v_sel = v_bh[b_idx, h_idx, sel[..., j]]
            out = out + jnp.einsum('bqhk,bqhkd->bqhd', p_parts[j], v_sel)
        return out

    outs = lax.map(attend_chunk, jnp.arange(seq // Q_BLOCK))
    o = outs.transpose(1, 0, 2, 3, 4).reshape(bsz, seq, ATTN_WIDTH_2).astype(h.dtype)
    return o @ w_out

def second_inputs(seed: int = 0) -> dict:
    key = jax.random.key(seed)
    ks = jax.random.split(key, 24)
    f32 = jnp.float32
    nrm = lambda k, shape, scale: jax.random.normal(k, shape, f32) * scale
    x = nrm(ks[0], (BATCH, SEQ, D_MODEL), 1.0)
    ffn_norm = 1.0 + nrm(ks[1], (DEPTH_2, 2, D_MODEL), 0.02)
    ffn_w_gate = nrm(ks[2], (DEPTH_2, 2, D_MODEL, D_FF), D_MODEL ** -0.5)
    ffn_w_up = nrm(ks[3], (DEPTH_2, 2, D_MODEL, D_FF), D_MODEL ** -0.5)
    ffn_w_down = nrm(ks[4], (DEPTH_2, 2, D_FF, D_MODEL), D_FF ** -0.5)
    mix_norm = 1.0 + nrm(ks[5], (DEPTH_2, D_MODEL), 0.02)
    s5_w_in = nrm(ks[6], (N_A, D_MODEL, S5_WIDTH), D_MODEL ** -0.5)
    s5_a_re = -0.5 + nrm(ks[7], (N_A, S5_GROUPS, S5_STATE), 0.01)
    s5_a_im = math.pi * jnp.arange(S5_STATE, dtype=f32)[None, None, :] + nrm(ks[8], (N_A, S5_GROUPS, S5_STATE), 0.01)
    s5_log_dt = jax.random.uniform(ks[9], (N_A, S5_GROUPS), f32, math.log(S5_DT_MIN), math.log(S5_DT_MAX))
    s5_b_re = nrm(ks[10], (N_A, S5_GROUPS, S5_STATE, S5_GROUP), (2 * S5_GROUP) ** -0.5)
    s5_b_im = nrm(ks[11], (N_A, S5_GROUPS, S5_STATE, S5_GROUP), (2 * S5_GROUP) ** -0.5)
    s5_c_re = nrm(ks[12], (N_A, S5_GROUPS, S5_GROUP, S5_STATE), S5_STATE ** -0.5)
    s5_c_im = nrm(ks[13], (N_A, S5_GROUPS, S5_GROUP, S5_STATE), S5_STATE ** -0.5)
    s5_d = nrm(ks[14], (N_A, S5_WIDTH), 1.0)
    s5_w_glu = nrm(ks[15], (N_A, S5_WIDTH, S5_WIDTH), S5_WIDTH ** -0.5)
    s5_w_out = nrm(ks[16], (N_A, S5_WIDTH, D_MODEL), S5_WIDTH ** -0.5)
    moba_w_qkv = nrm(ks[17], (N_B, D_MODEL, 3 * ATTN_WIDTH_2), D_MODEL ** -0.5)
    moba_q_norm = 1.0 + nrm(ks[18], (N_B, HEAD_DIM_2), 0.02)
    moba_k_norm = 1.0 + nrm(ks[19], (N_B, HEAD_DIM_2), 0.02)
    moba_w_out = nrm(ks[20], (N_B, ATTN_WIDTH_2, D_MODEL), ATTN_WIDTH_2 ** -0.5)
    return {'x': x, 'ffn_norm': ffn_norm, 'ffn_w_gate': ffn_w_gate, 'ffn_w_up': ffn_w_up,
            'ffn_w_down': ffn_w_down, 'mix_norm': mix_norm, 's5_w_in': s5_w_in,
            's5_a_re': s5_a_re, 's5_a_im': s5_a_im, 's5_log_dt': s5_log_dt,
            's5_b_re': s5_b_re, 's5_b_im': s5_b_im, 's5_c_re': s5_c_re, 's5_c_im': s5_c_im,
            's5_d': s5_d, 's5_w_glu': s5_w_glu, 's5_w_out': s5_w_out,
            'moba_w_qkv': moba_w_qkv, 'moba_q_norm': moba_q_norm, 'moba_k_norm': moba_k_norm,
            'moba_w_out': moba_w_out}

def second_block(x, ffn_norm, ffn_w_gate, ffn_w_up, ffn_w_down, mix_norm, s5_w_in,
              s5_a_re, s5_a_im, s5_log_dt, s5_b_re, s5_b_im, s5_c_re, s5_c_im,
              s5_d, s5_w_glu, s5_w_out, moba_w_qkv, moba_q_norm, moba_k_norm, moba_w_out):
    h = x
    for layer in range(DEPTH_2):
        h = h + MACARON_WEIGHT * swiglu(rms_norm_2(h, ffn_norm[layer, 0]), ffn_w_gate[layer, 0],
                                        ffn_w_up[layer, 0], ffn_w_down[layer, 0])
        hn = rms_norm_2(h, mix_norm[layer])
        i = layer // N_MIXERS
        if layer % N_MIXERS == 0:
            h = h + s5_mixer(hn, s5_w_in[i], s5_a_re[i], s5_a_im[i], s5_log_dt[i], s5_b_re[i],
                             s5_b_im[i], s5_c_re[i], s5_c_im[i], s5_d[i], s5_w_glu[i], s5_w_out[i])
        else:
            h = h + moba_mixer(hn, moba_w_qkv[i], moba_q_norm[i], moba_k_norm[i], moba_w_out[i])
        h = h + MACARON_WEIGHT * swiglu(rms_norm_2(h, ffn_norm[layer, 1]), ffn_w_gate[layer, 1],
                                        ffn_w_up[layer, 1], ffn_w_down[layer, 1])
    return h


def setup_inputs(seed=0):
    out = dict(first_inputs(seed))
    for name, value in second_inputs(seed + 1).items():
        if name != "x":
            out[name + "_2"] = value
    return out


def reference(
    x, c, w_ada, b_ada, g_norm1, w_in, g_q, g_k, g_ik, w_pool_grp, s_pool, w_up_attn, w_up_pool,
    w_out, g_norm2, w_peer_q, peer_subkeys, peer_u, peer_v, ffn_norm_2, ffn_w_gate_2,
    ffn_w_up_2, ffn_w_down_2, mix_norm_2, s5_w_in_2, s5_a_re_2, s5_a_im_2, s5_log_dt_2,
    s5_b_re_2, s5_b_im_2, s5_c_re_2, s5_c_im_2, s5_d_2, s5_w_glu_2, s5_w_out_2, moba_w_qkv_2,
    moba_q_norm_2, moba_k_norm_2, moba_w_out_2,
):
    x = first_block(
        x, c, w_ada, b_ada, g_norm1, w_in, g_q, g_k, g_ik, w_pool_grp, s_pool, w_up_attn,
        w_up_pool, w_out, g_norm2, w_peer_q, peer_subkeys, peer_u, peer_v,
    )
    return second_block(
        x, ffn_norm_2, ffn_w_gate_2, ffn_w_up_2, ffn_w_down_2, mix_norm_2, s5_w_in_2, s5_a_re_2,
        s5_a_im_2, s5_log_dt_2, s5_b_re_2, s5_b_im_2, s5_c_re_2, s5_c_im_2, s5_d_2, s5_w_glu_2,
        s5_w_out_2, moba_w_qkv_2, moba_q_norm_2, moba_k_norm_2, moba_w_out_2,
    )


_drawn_inputs = setup_inputs


def setup_inputs(seed=0):
    import zlib

    import numpy as np

    out = dict(_drawn_inputs(seed))
    spreads = {}
    factors = {'g_norm1': 2.914,
     'g_q': 8.0,
     'g_k': 8.0,
     'g_ik': 4.483,
     'ffn_norm_2': 3.695,
     'mix_norm_2': 6.15,
     's5_a_re_2': 8.0,
     's5_b_re_2': 3.077,
     's5_b_im_2': 3.013,
     's5_c_re_2': 3.144,
     's5_c_im_2': 3.063,
     'moba_q_norm_2': 8.0,
     'moba_k_norm_2': 8.0}
    for name, (base, spread) in spreads.items():
        noise = np.random.default_rng([zlib.crc32(name.encode()), seed]).standard_normal(out[name].shape)
        drawn = base * np.exp(spread * noise) if base else spread * noise
        out[name] = __import__('jax').numpy.asarray(drawn.astype(out[name].dtype))
    for name, factor in factors.items():
        out[name] = (out[name] * factor).astype(out[name].dtype)
    return out
```

```python
from contextlib import ExitStack

import numpy as np

import concourse.bass as bass
from concourse import mybir

F32 = mybir.dt.float32
U32 = mybir.dt.uint32
ALU = mybir.AluOpType
ACT = mybir.ActivationFunctionType
AX_X = mybir.AxisListType.X

P = 128
D = 1024
DC = D // P
T = 256
TT = T // P
EPS = 1e-6
NEG = -1e30
GONE = -3e38

NH, HD = 8, 64
IH = 4
TOPK = min(256, T // 4)
NATQ = NH * HD
NATW = NATQ + 3 * HD + IH
PH, PK, NKEYS = 8, 16, 128
NSLOT = PH * PK
UVB = 8
FF = 2816
FU = FF // P
SG, SP_, SN = 64, 64, 16
NPAIR = SG // 2
HALF = T // 2
MH, MD = 8, 128
ROT = MD // 8

NS = 4
SLOT = 3072
TWO_PI = 6.283185
MAGIC = 12582912.0


def unit_plan():
    plan = []

    def add(name, n, words):
        plan.extend((name, i, words) for i in range(n))

    add("ada", 16, 3 * DC * P)
    add("nat", 2, DC // 2 * NATW)
    add("tz", 3, 2 * DC * P)
    add("zg", 8, 2 * DC * P)
    add("up", 4, 2 * DC * P)
    add("wo", 4, 2 * D)
    add("pq", 4, 2 * DC * P)
    add("ffn0", FU, SLOT)
    add("s5in", 4, 2 * DC * P)
    add("s5b", 8, 4 * 4 * P)
    add("glu", 4, 2 * DC * P)
    add("s5out", 4, 2 * D)
    add("ffn1", FU, SLOT)
    add("ffn2", FU, SLOT)
    add("qkv", 12, 4 * 512)
    add("mo", 4, 2 * D)
    add("ffn3", FU, SLOT)
    return plan


PLAN = unit_plan()
UNIT = {(name, i): u for u, (name, i, _) in enumerate(PLAN)}
TWO_CHUNKS = ("tz", "zg", "up", "pq", "s5in", "glu")
HALVES = {}
for _name, _i, _ in PLAN:
    if _name in TWO_CHUNKS:
        HALVES[(_name, _i)] = len(HALVES)

COLS = {}
_at = 0
for _name, _n in (("c", DC), ("b_ada", 6 * DC), ("g1", DC), ("g2", DC), ("gain", 6 * DC), ("s_pool", 4),
                  ("d_skip", DC), ("a_re", NPAIR), ("a_im", NPAIR), ("log_dt", NPAIR)):
    COLS[_name] = (_at, _at + _n)
    _at += _n
NCOL = _at


class Count:

    def __init__(self):
        self.n = {}

    def up(self, sem):
        self.n[sem.name] = self.n.get(sem.name, 0) + 1
        return self.n[sem.name]


def build(nc, a, out):
    ctx = ExitStack()
    with ctx:
        def sb(name, shape, dt=F32):
            return ctx.enter_context(nc.sbuf_tensor(name, shape, dt))

        def sem(name):
            return ctx.enter_context(nc.semaphore(name))

        ring = sb("ring", [P, NS, SLOT])
        X = sb("X", [P, TT, D])
        XN = sb("XN", [P, TT, D])
        hT = sb("hT", [P, DC, T])
        ident = sb("ident", [P, P])
        zeros = sb("zeros", [P, P])
        cols = sb("cols", [P, NCOL])
        rows = sb("rows", [P, 3 * HD + 2 * MD])
        rope = sb("rope", [P, TT, 2, ROT])
        ada = sb("ada", [P, 6, DC])
        A1 = sb("A1", [P, DC])
        A2 = sb("A2", [P, DC])
        stat = sb("stat", [P, 16])
        hstat = sb("hstat", [P, 4, 32])
        act_gs = sb("act_gs", [P, 2, T])
        act_a = sb("act_a", [P, 2, T])
        s5p = sb("s5p", [P, 16, NPAIR])
        base_t = sb("base_t", [P, 4, NPAIR, 16])
        arena = sb("arena", [P, 28672])

        def part(at, *shape):
            n = int(np.prod(shape))
            v = arena[:, at:at + n]
            if len(shape) == 2:
                v = v.rearrange("p (a b) -> p a b", b=shape[1])
            if len(shape) == 3:
                v = v.rearrange("p (a b c) -> p a b c", b=shape[1], c=shape[2])
            return v

        brow = part(0, 4, D)
        zq = part(4096, TT, 12, HD)
        sq = part(5632, TT, 12, HD)
        vn = part(7168, TT, HD)
        iw = part(7296, TT, IH)
        qkT = part(7304, 6, T)
        iqT = part(8840, 2, T)
        PW = 16 + T
        pT = part(9352, 4, PW)
        pw0 = part(10440, 4, PW)
        pw1 = part(11528, 4, PW)
        rel = part(12616, 4, T)
        score = part(13640, 2, T)
        maskb = part(14152, TT, T)
        sg = part(14664, 16, T)
        L = part(18760, NH, T)
        PT = part(20808, 2, 2, 4 * P)
        yat = part(22856, 4, T)
        ypT = part(23880, 4, T)
        mixT = part(24904, DC, T)
        tmp = part(26952, 2, 512)
        rcnt = part(26952, 4, T)
        wgrp = part(27976, 4, P)
        skd = part(4096, PH, 2 * NKEYS)
        pqT = part(6144, DC, T)
        sco = part(8192, TT, 16, NKEYS)
        cand = part(12288, PH, PK * PK)
        oneh = part(14336, NSLOT, PK)
        uv = [part(16384 + 2048 * j, 2, D) for j in range(6)] + [part(4096 + 2048 * j, 2, D) for j in range(2)]
        Ec = part(0, NPAIR, HALF)
        Es = part(4096, NPAIR, HALF)
        et0 = part(8192, NPAIR, HALF)
        et1 = part(12288, NPAIR, HALF)
        cri = part(16384, 2, NPAIR, SN)
        crt = part(17408, 2, NPAIR, SN)
        CC = part(18432, 3, NPAIR, 2 * SN)
        uT = part(21504, DC, T)
        s5w = part(8192, 14, 4, HALF)
        yT = part(23552, DC, T)
        gT = part(25600, DC, T)
        qkv = part(0, TT, 24, MD)
        msq = part(6144, 2, 16, MD)
        mrt = part(10240, 4, TT * 16, ROT)
        mqT = part(12288, MH, T)
        mkT = part(14336, MH, T)
        mL = part(16384, MH, T)
        mPT = part(18432, 2, 2, 4 * P)
        moT = part(20480, MH, T)
        causal = part(22528, P)

        hflat = hT[:, :, :].rearrange("p a b -> p (a b)")

        def hpart(at, a_, b_):
            return hflat[:, at:at + a_ * b_].rearrange("p (a b) -> p a b", b=b_)

        tv = hpart(0, 16, PK)
        ti = hpart(256, 16, PK).bitcast(U32)
        tif = hpart(512, 16, PK)
        work = hflat[:, 768:1024]
        bv = hpart(1024, PH, PK)
        bp = hflat[:, 1152:1280].bitcast(U32)
        bq = hpart(1280, 2, NSLOT).bitcast(U32)
        bqf = hpart(1536, 2, NSLOT)
        ei = hpart(1792, 2, NSLOT)
        diag = hpart(0, UVB, P)
        eidx = sb("eidx", [P, TT, NSLOT], U32)
        gate = sb("gate", [P, TT, PH, PK])
        gst = sb("gst", [P, 2, PH])
        iota16 = sb("iota16", [P, PK])
        iotai = sb("iotai", [P, T], U32)
        ibuf = sb("ibuf", [P, UVB], U32)
        dots = sb("dots", [P, UVB])
        gl = sb("gl", [P, UVB])
        top8 = sb("top8", [P, 8])
        rmax = sb("rmax", [P, 4, NH])

        PB = [ctx.enter_context(nc.psum_tensor(f"PB{b}", [P, 512], F32)) for b in range(8)]

        x_here = sem("x_here")
        small_here = sem("small_here")
        sk_here = sem("sk_here")
        c_here = sem("c_here")
        w_here = [sem(f"w_here{s}") for s in range(NS)]
        unit_done = sem("unit_done")
        half_done = sem("half_done")
        ident_ready = sem("ident_ready")
        dve_link, act_link, pool_link = sem("dve_link"), sem("act_link"), sem("pool_link")
        ada_ready = sem("ada_ready")
        brow_full, brow_done = sem("brow_full"), sem("brow_done")
        var_ready, root_ready, rstd_ready = sem("var_ready"), sem("root_ready"), sem("rstd_ready")
        xn_act, xn_dve, h2_ready = sem("xn_act"), sem("xn_dve"), sem("h2_ready")
        tr_full, hT_dve, hT_act = sem("tr_full"), sem("hT_dve"), sem("hT_act")
        natq_out, nat_out = sem("natq_out"), sem("nat_out")
        hvar_ready, hroot_ready, qk_ready = sem("hvar_ready"), sem("hroot_ready"), sem("qk_ready")
        tz_done = sem("tz_done")
        qkT_full, qkT_done = sem("qkT_full"), sem("qkT_done")
        idx_full, rel_done, mask_ready = sem("idx_full"), sem("rel_done"), sem("mask_ready")
        lg_full, L_done, nm_ready, exp_done, p_ready = (sem("lg_full"), sem("L_done"), sem("nm_ready"),
                                                        sem("exp_done"), sem("p_ready"))
        pt_full, pt_act, pt_dve = sem("pt_full"), sem("pt_act"), sem("pt_dve")
        av_full, av_done = sem("av_full"), sem("av_done")
        mixp_ready, pg_full, pg_done = sem("mixp_ready"), sem("pg_full"), sem("pg_done")
        rcnt_ready = sem("rcnt_ready")
        mixT_done = sem("mixT_done")
        x_done = sem("x_done")
        pq_done = sem("pq_done")
        sc_full, sc_done = sem("sc_full"), sem("sc_done")
        gx_ready, ge_done, route_ready = sem("gx_ready"), sem("ge_done"), sem("route_ready")
        idx_copied = sem("idx_copied")
        uv_here = [sem(f"uv_here{j}") for j in range(UVB)]
        dot_done, gelu_done, diag_done, uv_used = sem("dot_done"), sem("gelu_done"), sem("diag_done"), sem("uv_used")
        gu_done, silu_done, a_done = sem("gu_done"), sem("silu_done"), sem("a_done")
        ang_ready, trig_ready, s5p_ready = sem("ang_ready"), sem("trig_ready"), sem("s5p_ready")
        tab_ready = sem("tab_ready")
        u_done, bu_full, v_parts, v_ready = sem("u_done"), sem("bu_full"), sem("v_parts"), sem("v_ready")
        w_ready, o_ready, y_full, y_done = sem("w_ready"), sem("o_ready"), sem("y_full"), sem("y_done")
        g_ready, sig_done, g2_done = sem("g_ready"), sem("sig_done"), sem("g2_done")
        mq_act, mq_dve = sem("mq_act"), sem("mq_dve")
        causal_ready = sem("causal_ready")
        mqT_full, mqT_act, mqT_dve = sem("mqT_full"), sem("mqT_act"), sem("mqT_dve")
        stored = sem("stored")

        def col(name):
            return cols[:, COLS[name][0]:COLS[name][1]]

        def w_chunk(u, c, k, kn=DC):
            o = (c * kn + k) * P
            return ring[:, u % NS, o:o + P]

        ffn_base = [UNIT[(f"ffn{f}", 0)] for f in range(4)]
        LOOPS = FU // NS
        N_FFN, N_S5, N_MOBA = (2, 4, 5, 7), 3, 6

        block = ctx.enter_context(nc.Block())

        @block.sync
        def _(sp):
            def load(name, n):
                for i in range(n):
                    u = UNIT[(name, i)]
                    words = PLAN[u][2]
                    if u >= NS:
                        sp.wait_ge(unit_done, u - NS + 1)
                    sp.dma_start(ring[:, u % NS, 0:words], a[name][i]).then_inc(w_here[u % NS], 16)

            def load_ffn(f):
                w = a["ffn"].rearrange("u p w -> (u p) w")
                u0 = ffn_base[f]

                def one(j, row):
                    sp.dma_start(ring[:, (u0 + j) % NS, :], w[bass.ds(row, P), :]).then_inc(
                        w_here[(u0 + j) % NS], 16)

                with sp.Fori(0, LOOPS) as i:
                    for j in range(NS):
                        sp.wait_ge(unit_done, i * NS + (u0 + j - NS + 1))
                        one(j, i * (NS * P) + (f * FU + j) * P)
                for j in range(LOOPS * NS, FU):
                    sp.wait_ge(unit_done, u0 + j - NS + 1)
                    one(j, (f * FU + j) * P)

            load("ada", 16)
            load("nat", 2)
            load("tz", 3)
            load("zg", 8)
            load("up", 4)
            load("wo", 4)
            load("pq", 4)
            load_ffn(0)
            load("s5in", 4)
            load("s5b", 8)
            load("glu", 4)
            load("s5out", 4)
            load_ffn(1)
            load_ffn(2)
            load("qkv", 12)
            load("mo", 4)
            load_ffn(3)
            sp.wait_ge(x_done, 4 * 8)
            sp.dma_start(out.rearrange("(t p) d -> p t d", p=P), X[:, :, :]).then_inc(stored, 16)
            sp.wait_ge(stored, 16)

        @block.tensor
        def _(pe):
            def here(u):
                pe.wait_ge(w_here[u % NS], 16 * (u // NS + 1))

            def h_ready(n):
                pe.wait_ge(hT_dve, 4 * (n + 1))
                pe.wait_ge(hT_act, 4 * (n + 1))

            def transposes(n):
                if n == 1:
                    pe.wait_ge(h2_ready, TT)
                else:
                    pe.wait_ge(xn_act, n + 1)
                    pe.wait_ge(xn_dve, n + 1)
                for q in range(4):
                    if q == 2:
                        pe.wait_ge(hT_dve, 4 * n + 2)
                    if q == 3:
                        pe.wait_ge(hT_act, 4 * n + 2)
                    for j in range(2):
                        for t in range(TT):
                            dc = 2 * q + j
                            mm = pe.transpose(PB[6 + q % 2][:, j * T + t * P:j * T + (t + 1) * P],
                                              XN[:, t, dc * P:(dc + 1) * P], ident[:, :])
                    mm.then_inc(tr_full, 1)

            def chunks(name, n, src, banks_free):
                for i in range(n):
                    u = UNIT[(name, i)]
                    here(u)
                    for c in range(2):
                        banks_free(2 * i + c)
                        for k in range(DC):
                            mm = pe.matmul(PB[c][:, 0:T], lhsT=w_chunk(u, c, k), rhs=src[:, k, :],
                                           start=(k == 0), stop=(k == DC - 1))
                        mm.then_inc(half_done if c == 0 else unit_done, 1)

            def natural(name, src):
                for i in range(4):
                    u = UNIT[(name, i)]
                    here(u)
                    for kk in range(2):
                        k = 2 * i + kk
                        for t in range(TT):
                            for n in range(2):
                                mm = pe.matmul(PB[2 + 2 * t + n][:, :], lhsT=src[:, k, t * P:(t + 1) * P],
                                               rhs=ring[:, u % NS, kk * D + n * 512:kk * D + (n + 1) * 512],
                                               start=(k == 0), stop=(k == DC - 1))
                    mm.then_inc(unit_done, 1)

            def free01(done, before):
                def wait(c):
                    if before + c >= 2:
                        pe.wait_ge(done, before + c - 1)
                return wait

            pe.wait_ge(small_here, 16 * 4)
            cc = col("c")
            for i in range(16):
                u = UNIT[("ada", i)]
                here(u)
                for c in range(3):
                    for k in range(DC):
                        mm = pe.matmul(PB[6][:, 3 * i + c:3 * i + c + 1], lhsT=w_chunk(u, c, k),
                                       rhs=cc[:, k:k + 1], start=(k == 0), stop=(k == DC - 1))
                mm.then_inc(unit_done, 1)
            pe.wait_ge(ident_ready, 1)
            pe.wait_ge(ada_ready, 3)
            for i in range(8):
                if i >= 4:
                    pe.wait_ge(brow_done, i - 3)
                src = (ada[:, 2, :], A2[:, :], ada[:, 3, :], ada[:, 5, :])[i // 2]
                for j in range(4):
                    c = 4 * (i % 2) + j
                    mm = pe.matmul(PB[2 + i % 4][:, j * P:(j + 1) * P], lhsT=src[:, c:c + 1].broadcast_to([P, P]),
                                   rhs=ident[:, :], start=True, stop=True)
                mm.then_inc(brow_full, 1)
            transposes(0)
            h_ready(0)
            pe.wait_ge(brow_done, 8)
            for i in range(2):
                u = UNIT[("nat", i)]
                here(u)
                for kk in range(4):
                    k = 4 * i + kk
                    for t in range(TT):
                        for b, lo, hi in ((2, 0, NATQ), (4, NATQ, NATW)):
                            mm = pe.matmul(PB[b + t][:, 0:hi - lo], lhsT=hT[:, k, t * P:(t + 1) * P],
                                           rhs=ring[:, u % NS, kk * NATW + lo:kk * NATW + hi],
                                           start=(k == 0), stop=(k == DC - 1))
                mm.then_inc(unit_done, 1)
            chunks("tz", 3, hT, free01(tz_done, 0))

            def gates(i0, i1):
                for i in range(i0, i1):
                    u = UNIT[("zg", i)]
                    here(u)
                    for c in range(2):
                        pe.wait_ge(tz_done, 6 + 2 * i + c - 1)
                        for k in range(DC):
                            mm = pe.matmul(PB[c][:, 0:T], lhsT=w_chunk(u, c, k), rhs=hT[:, k, :],
                                           start=(k == 0), stop=(k == DC - 1))
                        mm.then_inc(half_done if c == 0 else unit_done, 1)

            gates(0, 4)
            pe.wait_ge(qk_ready, 1)
            for p in range(6):
                if p >= 2:
                    pe.wait_ge(qkT_done, p - 1)
                for t in range(TT):
                    mm = pe.transpose(PB[6 + p % 2][:, t * P:(t + 1) * P],
                                      zq[:, t, 2 * p:2 * p + 2, :].rearrange("p a b -> p (a b)"), ident[:, :])
                mm.then_inc(qkT_full, 1)
            pe.wait_ge(qkT_done, 6)
            pe.wait_ge(tz_done, 2)
            pe.wait_ge(nat_out, 2)
            pe.wait_ge(natq_out, 2)
            for t in range(TT):
                S = (t + 1) * P
                for h in range(IH):
                    r, o = h % 2, (h // 2) * T
                    mm = pe.matmul(PB[2 + 2 * t + r][:, o:o + S], lhsT=iqT[r * HD:(r + 1) * HD, h // 2, t * P:(t + 1) * P],
                                   rhs=qkT[r * HD:(r + 1) * HD, 5, 0:S], start=True, stop=True)
                mm.then_inc(idx_full, 1)
            gates(4, 8)
            pe.wait_ge(mixp_ready, 1)
            for g in range(4):
                if g < 2:
                    pe.wait_ge(tz_done, 21 + g)
                else:
                    pe.wait_ge(pg_done, g - 1)
                pe.matmul(PB[g % 2][:, 0:T], lhsT=wgrp[:, g, :], rhs=pw0[:, g, 0:T],
                          start=True, stop=True).then_inc(pg_full, 1)
            for t in range(TT):
                S = (t + 1) * P
                pe.wait_ge(rel_done, 4)
                if t:
                    pe.wait_ge(L_done, 4)
                for h in range(NH):
                    r, j = h % 2, h // 2
                    mm = pe.matmul(PB[2 + r + 2 * (j // 2)][:, (j % 2) * T:(j % 2) * T + S],
                                   lhsT=qkT[r * HD:(r + 1) * HD, j, t * P:(t + 1) * P],
                                   rhs=qkT[r * HD:(r + 1) * HD, 4, 0:S], start=True, stop=True)
                mm.then_inc(lg_full, 1)
                pe.wait_ge(p_ready, t + 1)
                for s in range(t + 1):
                    if t + s > 0:
                        pe.wait_ge(pt_act, t + s)
                        pe.wait_ge(pt_dve, t + s)
                    for r in range(2):
                        for j in range(4):
                            mm = pe.transpose(PB[6 + r][:, j * P:(j + 1) * P], L[:, 2 * j + r, s * P:(s + 1) * P],
                                              ident[:, :])
                        mm.then_inc(pt_full, 1)
                if t == 0:
                    pe.wait_ge(pg_done, 4)
                pe.wait_ge(pt_act, t + t + 1)
                pe.wait_ge(pt_dve, t + t + 1)
                for s in range(t + 1):
                    for r in range(2):
                        mm = pe.matmul(PB[t][r * HD:(r + 1) * HD, :], lhsT=vn[:, s, :], rhs=PT[:, s, r, :],
                                       start=(s == 0), stop=(s == t), skip_group_check=True)
                mm.then_inc(av_full, 1)
            pe.wait_ge(av_done, 2)
            for i in range(4):
                u = UNIT[("up", i)]
                here(u)
                for c in range(2):
                    dc = 2 * i + c
                    if dc >= 2:
                        pe.wait_ge(mixT_done, dc - 1)
                    for b, src in enumerate((yat, ypT)):
                        for k in range(4):
                            mm = pe.matmul(PB[c][:, b * T:(b + 1) * T], lhsT=w_chunk(u, c, 4 * b + k),
                                           rhs=src[:, k, :], start=(k == 0), stop=(k == 3))
                    mm.then_inc(half_done if c == 0 else unit_done, 1)
            pe.wait_ge(mixT_done, DC)
            natural("wo", mixT)
            transposes(1)
            h_ready(1)
            chunks("pq", 4, hT, lambda c: pe.wait_ge(pq_done, c - 1) if c >= 2 else None)
            pe.wait_ge(pq_done, 8)
            pe.wait_ge(sk_here, 16)
            pe.wait_ge(x_done, 4)
            for t in range(TT):
                for hp in range(4):
                    if t:
                        pe.wait_ge(sc_done, hp + 1)
                    for j in range(2):
                        h = 2 * hp + j
                        mm = pe.matmul(PB[2 + hp][:, j * 256:(j + 1) * 256], lhsT=pqT[:, h, t * P:(t + 1) * P],
                                       rhs=skd[:, h, :], start=True, stop=True)
                    mm.then_inc(sc_full, 1)
            pe.wait_ge(sc_done, 8)
            for t in range(TT):
                for n in range(2):
                    mm = pe.matmul(PB[2 + 2 * t + n][:, :], lhsT=zeros[:, :], rhs=XN[:, t, 0:512], start=True,
                                   stop=False, skip_group_check=True)
                if t == 0:
                    mm.then_inc(uv_used, UVB)
                with pe.Fori(0, NSLOT // UVB) as i:
                    for j in range(UVB):
                        pe.wait_ge(diag_done, i * UVB + (t * NSLOT + j + 1))
                        for n in range(2):
                            mm = pe.matmul(PB[2 + 2 * t + n][:, :], lhsT=diag[:, j, :],
                                           rhs=uv[j][:, 1, n * 512:(n + 1) * 512], start=False, stop=False,
                                           skip_group_check=True)
                        mm.then_inc(uv_used, 1)

            def ffn(f):
                n, u0, a0 = N_FFN[f], ffn_base[f], FU * f

                def gate_up(j, i=None):
                    u = u0 + j
                    if i is None:
                        pe.wait_ge(w_here[u % NS], 16 * (u // NS + 1))
                        pe.wait_ge(a_done, a0 + j + 1)
                    else:
                        pe.wait_ge(w_here[u % NS], i * 16 + 16 * (u // NS + 1))
                        pe.wait_ge(a_done, i * NS + (a0 + j + 1))
                    for b in range(2):
                        for k in range(DC):
                            mm = pe.matmul(PB[j % 2][:, b * T:(b + 1) * T], lhsT=w_chunk(u, b, k), rhs=hT[:, k, :],
                                           start=(k == 0), stop=(k == DC - 1))
                    mm.then_inc(gu_done, 1)

                def down(j, i=None, start=False, stop=False):
                    u = u0 + j
                    if i is None:
                        pe.wait_ge(a_done, a0 + j + 3)
                    else:
                        pe.wait_ge(a_done, i * NS + (a0 + j + 3))
                    for t in range(TT):
                        for h in range(2):
                            mm = pe.matmul(PB[2 + 2 * t + h][:, :], lhsT=act_a[:, j % 2, t * P:(t + 1) * P],
                                           rhs=ring[:, u % NS, 2 * D + h * 512:2 * D + (h + 1) * 512],
                                           start=start, stop=stop, skip_group_check=True)
                    mm.then_inc(unit_done, 1)

                transposes(n)
                h_ready(n)
                gate_up(0)
                for t in range(TT):
                    for h in range(2):
                        pe.matmul(PB[2 + 2 * t + h][:, :], lhsT=zeros[:, :], rhs=X[:, t, 0:512],
                                  start=True, stop=False, skip_group_check=True)
                with pe.Fori(0, LOOPS) as i:
                    for j in range(NS):
                        gate_up(j + 1, i)
                        down(j, i)
                for j in range(LOOPS * NS, FU):
                    if j + 1 < FU:
                        gate_up(j + 1)
                    down(j, stop=(j == FU - 1))

            ffn(0)
            transposes(N_S5)
            h_ready(N_S5)
            pe.wait_ge(a_done, FU + 2)
            chunks("s5in", 4, hT, lambda c: pe.wait_ge(u_done, c - 1) if c >= 2 else None)
            pe.wait_ge(u_done, 8)
            pe.wait_ge(x_done, 12)
            pe.wait_ge(tab_ready, 2)

            def s5_in(i):
                half, q = i // 8, i % 8
                u = UNIT[("s5b", i // 2)]
                if q % 2 == 0:
                    here(u)
                if i >= 2:
                    pe.wait_ge(v_parts, i - 1)
                for b in range(2):
                    for j in range(4):
                        o = (((q % 2) * 2 + b) * 4 + j) * P
                        mm = pe.matmul(PB[2 + 2 * (i % 2) + b][:, j * P:(j + 1) * P], lhsT=ring[:, u % NS, o:o + P],
                                       rhs=uT[:, q, half * HALF:(half + 1) * HALF], start=True, stop=True)
                    if b == 0 and q % 2 == 1:
                        continue
                if q % 2 == 0:
                    mm.then_inc(bu_full, 1)
                else:
                    mm.then_inc(unit_done, 1)

            def s5_out(i):
                q = i % 8
                pe.wait_ge(o_ready, i + 1)
                if i >= 2:
                    pe.wait_ge(y_done, i - 1)
                for j in range(4):
                    for m, (c, o) in enumerate(((0, 0), (1, 1), (2, 2), (2, 3))):
                        mm = pe.matmul(PB[6 + i % 2][32 * j:32 * j + 32, 0:HALF],
                                       lhsT=CC[:, c, 4 * q + j, :], rhs=s5w[:, 4 + 4 * (i % 2) + o, j, :],
                                       start=(m == 0), stop=(m == 3), skip_group_check=True)
                mm.then_inc(y_full, 1)

            s5_in(0)
            for i in range(16):
                if i + 1 < 16:
                    s5_in(i + 1)
                s5_out(i)
            pe.wait_ge(g_ready, 1)
            chunks("glu", 4, gT, lambda c: pe.wait_ge(sig_done, c - 1) if c >= 2 else None)
            pe.wait_ge(g2_done, 8)
            natural("s5out", yT)
            ffn(1)
            ffn(2)
            transposes(N_MOBA)
            h_ready(N_MOBA)
            for m in range(6):
                if m >= 2:
                    pe.wait_ge(mq_act, m - 1)
                    pe.wait_ge(mq_dve, m - 1)
                for i in range(2):
                    u = UNIT[("qkv", 2 * m + i)]
                    here(u)
                    for kk in range(4):
                        k = 4 * i + kk
                        for t in range(TT):
                            mm = pe.matmul(PB[2 + 2 * (m % 2) + t][:, :], lhsT=hT[:, k, t * P:(t + 1) * P],
                                           rhs=ring[:, u % NS, kk * 512:(kk + 1) * 512],
                                           start=(k == 0), stop=(k == DC - 1))
                    mm.then_inc(unit_done, 1)
            pe.wait_ge(qk_ready, 2)
            for i in range(8):
                if i >= 2:
                    pe.wait_ge(mqT_dve if i % 2 else mqT_act, i // 2)
                for j in range(2):
                    for t in range(TT):
                        mm = pe.transpose(PB[6 + i % 2][:, j * T + t * P:j * T + (t + 1) * P],
                                          qkv[:, t, 2 * i + j, :], ident[:, :])
                mm.then_inc(mqT_full, 1)
            pe.wait_ge(mqT_act, 4)
            pe.wait_ge(mqT_dve, 4)
            pe.wait_ge(mq_act, 6)
            pe.wait_ge(mq_dve, 6)
            for t in range(TT):
                S = (t + 1) * P
                if t:
                    pe.wait_ge(L_done, 12)
                for h in range(MH):
                    mm = pe.matmul(PB[2 + h // 2][:, (h % 2) * T:(h % 2) * T + S], lhsT=mqT[:, h, t * P:(t + 1) * P],
                                   rhs=mkT[:, h, 0:S], start=True, stop=True)
                mm.then_inc(lg_full, 1)
                pe.wait_ge(p_ready, 3 + t)
                for s in range(t + 1):
                    if t + s > 0:
                        pe.wait_ge(pt_act, 3 + t + s)
                        pe.wait_ge(pt_dve, 3 + t + s)
                    for r in range(2):
                        for j in range(4):
                            mm = pe.transpose(PB[6 + r][:, j * P:(j + 1) * P], mL[:, 4 * r + j, s * P:(s + 1) * P],
                                              ident[:, :])
                        mm.then_inc(pt_full, 1)
                pe.wait_ge(pt_act, 4 + 2 * t)
                pe.wait_ge(pt_dve, 4 + 2 * t)
                if t:
                    pe.wait_ge(av_done, 3)
                for r in range(2):
                    for j in range(4):
                        for s in range(t + 1):
                            mm = pe.matmul(PB[r][:, j * P:(j + 1) * P], lhsT=qkv[:, s, 16 + 4 * r + j, :],
                                           rhs=mPT[:, s, r, j * P:(j + 1) * P], start=(s == 0), stop=(s == t))
                mm.then_inc(av_full, 1)
            pe.wait_ge(av_done, 4)
            natural("mo", moT)
            ffn(3)

        @block.vector
        def _(dve):
            v = nc.vector
            count = Count()

            def tell(ins, s):
                ins.then_inc(s, 1)
                dve.wait_ge(s, count.up(s))

            def link(ins):
                tell(ins, dve_link)

            def newton(r, root, var, tmp_, s):
                link(v.reciprocal(r, root))
                link(v.tensor_tensor(tmp_, r, r, ALU.mult))
                link(v.scalar_tensor_tensor(out=tmp_, in0=tmp_, scalar=-0.5, in1=var, op0=ALU.mult, op1=ALU.mult))
                tell(v.scalar_tensor_tensor(out=r, in0=tmp_, scalar=1.5, in1=r, op0=ALU.add, op1=ALU.mult), s)

            def norm(n):
                for t in range(TT):
                    link(v.tensor_tensor_reduce(out=XN[:, t, :], in0=X[:, t, :], in1=X[:, t, :], scale=1.0, scalar=0.0,
                                                op0=ALU.mult, op1=ALU.add, accum_out=stat[:, t:t + 1]))
                tell(v.tensor_scalar(stat[:, 2:4], stat[:, 0:2], 1.0 / D, EPS, ALU.mult, ALU.add), var_ready)
                dve.wait_ge(root_ready, n + 1)
                newton(stat[:, 6:8], stat[:, 4:6], stat[:, 2:4], stat[:, 8:10], rstd_ready)
                tell(v.tensor_scalar(XN[:, 1, :], X[:, 1, :], stat[:, 7:8], None, ALU.mult), xn_dve)

            def evac_h(n, scale, shift):
                for q in (0, 2):
                    dve.wait_ge(tr_full, 4 * n + q + 1)
                    for j in range(2):
                        dc = 2 * q + j
                        src = PB[6][:, j * T:(j + 1) * T]
                        if scale is None:
                            ins = v.tensor_copy(hT[:, dc, :], src)
                        elif shift is None:
                            ins = v.tensor_scalar(hT[:, dc, :], src, scale[:, dc:dc + 1], None, ALU.mult)
                        else:
                            ins = v.tensor_scalar(hT[:, dc, :], src, scale[:, dc:dc + 1], shift[:, dc:dc + 1],
                                                  ALU.mult, ALU.add)
                        tell(ins, hT_dve)

            def gain(n):
                return col("gain")[:, (n - 2) * DC:(n - 1) * DC]

            link(v.memset(zeros[:, :], 0.0))
            for j in range(2):
                tell(v.memset(act_a[:, j, :], 0.0), a_done)

            dve.wait_ge(small_here, 16 * 4)
            dve.wait_ge(ident_ready, 2)
            dt_, mag, f1, f16, f128 = (s5p[:, i, :] for i in range(5))
            t0, t1, t2 = s5p[:, 5, :], s5p[:, 6, :], s5p[:, 7, :]
            cf_re, cf_im, c128, s128 = s5p[:, 8, :], s5p[:, 9, :], s5p[:, 10, :], s5p[:, 11, :]

            def turn(x, scratch):
                link(v.tensor_scalar(scratch, x, MAGIC, MAGIC, ALU.add, ALU.subtract))
                link(v.tensor_tensor(x, x, scratch, ALU.subtract))

            dve.wait_ge(ang_ready, 1)
            link(v.tensor_tensor(t0, col("a_re"), dt_, ALU.mult))
            link(v.tensor_tensor(f1, col("a_im"), dt_, ALU.mult))
            link(v.tensor_scalar(f1, f1, 1.0 / (2.0 * np.pi), None, ALU.mult))
            turn(f1, t1)
            link(v.tensor_scalar(f16, f1, 16.0, None, ALU.mult))
            turn(f16, t1)
            link(v.tensor_scalar(f128, f1, float(HALF), None, ALU.mult))
            turn(f128, t1)
            sc4 = arena[:, 20000:20000 + NPAIR * 16].rearrange("p (a b) -> p a b", b=16)
            for b, f in ((0, f1), (2, f16)):
                m = 16 if b == 0 else 8
                link(v.tensor_tensor(base_t[:, b + 1, :, 0:m], f.unsqueeze(2).broadcast_to([P, NPAIR, m]),
                                     iota16[:, 0:m].unsqueeze(1).broadcast_to([P, NPAIR, m]), ALU.mult))
                link(v.tensor_scalar(base_t[:, b, :, 0:m], base_t[:, b + 1, :, 0:m], 0.25, None, ALU.add))
                turn(base_t[:, b, :, 0:m], sc4[:, :, 0:m])
                turn(base_t[:, b + 1, :, 0:m], sc4[:, :, 0:m])
            link(v.tensor_copy(s128, f128))
            link(v.tensor_scalar(c128, f128, 0.25, None, ALU.add))
            turn(c128, t1)
            tell(v.tensor_copy(t2, t0), s5p_ready)
            dve.wait_ge(trig_ready, 1)
            lre, lim = s5p[:, 12, :], s5p[:, 13, :]
            link(v.tensor_tensor(lre, mag, base_t[:, 0, :, 1], ALU.mult))
            link(v.tensor_tensor(lim, mag, base_t[:, 1, :, 1], ALU.mult))
            link(v.tensor_scalar(lre, lre, 1.0, None, ALU.subtract))
            link(v.tensor_tensor(t0, col("a_re"), col("a_re"), ALU.mult))
            link(v.tensor_tensor(t1, col("a_im"), col("a_im"), ALU.mult))
            link(v.tensor_tensor(t0, t0, t1, ALU.add))
            link(v.reciprocal(t2, t0))
            link(v.tensor_tensor(t0, lre, col("a_re"), ALU.mult))
            link(v.tensor_tensor(t1, lim, col("a_im"), ALU.mult))
            link(v.tensor_tensor(t0, t0, t1, ALU.add))
            link(v.tensor_tensor(cf_re, t0, t2, ALU.mult))
            link(v.tensor_tensor(t0, lim, col("a_re"), ALU.mult))
            link(v.tensor_tensor(t1, lre, col("a_im"), ALU.mult))
            link(v.tensor_tensor(t0, t0, t1, ALU.subtract))
            tell(v.tensor_tensor(cf_im, t0, t2, ALU.mult), s5p_ready)
            dve.wait_ge(ident_ready, 3)
            for g in range(4):
                link(v.tensor_scalar(rcnt[:, g, :], iotai[:, :], 2.0 ** (g + 1), None, ALU.min))
            tell(v.reciprocal(rcnt[:, :, :], rcnt[:, :, :]), rcnt_ready)

            dve.wait_ge(x_here, 16)
            norm(0)
            dve.wait_ge(unit_done, UNIT[("ada", 15)] + 1)
            tell(v.tensor_tensor(ada[:, :, :].rearrange("p a b -> p (a b)"), PB[6][:, 0:6 * DC], col("b_ada"), ALU.add),
                 ada_ready)
            tell(v.scalar_tensor_tensor(out=A1[:, :], in0=ada[:, 1, :], scalar=1.0, in1=col("g1"), op0=ALU.add,
                                        op1=ALU.mult), ada_ready)
            tell(v.scalar_tensor_tensor(out=A2[:, :], in0=ada[:, 4, :], scalar=1.0, in1=col("g2"), op0=ALU.add,
                                        op1=ALU.mult), ada_ready)
            evac_h(0, A1[:, :], ada[:, 0, :])

            dve.wait_ge(unit_done, UNIT[("nat", 1)] + 1)
            for t in range(TT):
                src = PB[4 + t]
                for c in range(4):
                    link(v.tensor_copy(zq[:, t, 8 + c, :], src[:, (c // 2) * HD:(c // 2 + 1) * HD]))
                link(v.tensor_copy(vn[:, t, :], src[:, 2 * HD:3 * HD]))
                tell(v.tensor_scalar(iw[:, t, :], src[:, 3 * HD:3 * HD + IH], IH ** -0.5, None, ALU.mult), nat_out)
            dve.wait_ge(natq_out, TT)

            def head_norm(z, z2, hd, nh, n):
                link(v.tensor_tensor(z2, z, z, ALU.mult))
                link(v.tensor_reduce(hstat[:, 0, 0:nh], z2, AX_X, ALU.add))
                tell(v.tensor_scalar(hstat[:, 0, 0:nh], hstat[:, 0, 0:nh], 1.0 / hd, EPS, ALU.mult, ALU.add), hvar_ready)
                dve.wait_ge(hroot_ready, n)
                newton(hstat[:, 2, 0:nh], hstat[:, 1, 0:nh], hstat[:, 0, 0:nh], hstat[:, 3, 0:nh], dve_link)
                link(v.tensor_tensor(z, z, hstat[:, 2, 0:nh].unsqueeze(2).broadcast_to([P, nh, hd]), ALU.mult))

            zf = zq.rearrange("p t h d -> p (t h) d")
            head_norm(zf, sq.rearrange("p t h d -> p (t h) d"), HD, 24, 1)
            for h0, h1, b in ((0, 8, 0), (8, 10, 1), (10, 12, 2)):
                zt = zq[:, :, h0:h1, :]
                gb = rows[:, b * HD:(b + 1) * HD].unsqueeze(1).unsqueeze(1).broadcast_to([P, TT, h1 - h0, HD])
                ins = v.tensor_tensor(zt, zt, gb, ALU.mult)
                if b < 2:
                    link(ins)
                else:
                    tell(ins, qk_ready)

            for t in range(TT):
                S = (t + 1) * P
                dve.wait_ge(rel_done, 2 * t + 2)
                sc0, sc1 = score[:, 0, 0:S], score[:, 1, 0:S]
                link(v.tensor_scalar(sc0, rel[:, 0, 0:S], iw[:, t, 0:1], None, ALU.mult))
                for plane, h in ((2, 1), (1, 2), (3, 3)):
                    link(v.scalar_tensor_tensor(out=sc0, in0=rel[:, plane, 0:S], scalar=iw[:, t, h:h + 1], in1=sc0,
                                                op0=ALU.mult, op1=ALU.add))
                link(v.memset(score[0:64, 0, S - 64:S], NEG))
                for r in range(TOPK // 8):
                    link(v.max(top8[:, :], sc0))
                    link(v.match_replace(out=sc0, in_to_replace=top8[:, :], in_values=sc0, imm_value=GONE))
                tell(v.tensor_scalar(maskb[:, t, 0:S], sc0, -2e38, NEG, ALU.is_gt, ALU.mult), mask_ready)

            def softmax_head(base, t, Lt, S, groups, scale, masks):
                dve.wait_ge(lg_full, base + t + 1)
                for g, dst in enumerate(groups):
                    masks(g, dst)
                link(v.tensor_reduce(rmax[:, 0, :], Lt[:, :, 0:S], AX_X, ALU.max))
                tell(v.tensor_scalar(rmax[:, 1, :], rmax[:, 0, :], -scale, None, ALU.mult), nm_ready)
                dve.wait_ge(exp_done, base + t + 1)
                link(v.reciprocal(rmax[:, 3, :], rmax[:, 2, :]))
                tell(v.tensor_tensor(Lt[:, :, 0:S], Lt[:, :, 0:S], rmax[:, 3, :].unsqueeze(2).broadcast_to([P, NH, S]),
                                     ALU.mult), p_ready)

            Lv = L.rearrange("p (jj hf r) s -> p jj hf r s", jj=2, hf=2)
            for t in range(TT):
                S = (t + 1) * P

                def masks(g, dst, S=S, t=t):
                    r, jj = g % 2, g // 2
                    src = PB[2 + g][:, :].rearrange("p (a s) -> p a s", a=2)[:, :, 0:S]
                    tell(v.tensor_tensor(Lv[:, jj, :, r, 0:S], src,
                                         maskb[:, t, 0:S].unsqueeze(1).broadcast_to([P, 2, S]), ALU.add), L_done)

                softmax_head(0, t, L, S, range(4), HD ** -0.5, masks)
                for s in range(t + 1):
                    dve.wait_ge(pt_full, 2 * (t + s) + 2)
                    tell(v.tensor_copy(PT[:, s, 1, :], PB[7][:, :]), pt_dve)
                dve.wait_ge(av_full, t + 1)
                tell(v.tensor_copy(yat[:, :, t * P:(t + 1) * P], PB[t][:, :].rearrange("p (j q) -> p j q", j=4)),
                     av_done)

            for dc in range(DC):
                i, c = dc // 2, dc % 2
                if c == 0:
                    dve.wait_ge(half_done, HALVES[("up", i)] + 1)
                else:
                    dve.wait_ge(unit_done, UNIT[("up", i)] + 1)
                link(v.tensor_tensor(tmp[:, 0, 0:T], PB[c][:, 0:T], sg[:, dc, :], ALU.mult))
                link(v.tensor_tensor(tmp[:, 1, 0:T], PB[c][:, T:2 * T], sg[:, DC + dc, :], ALU.mult))
                tell(v.tensor_tensor(mixT[:, dc, :], tmp[:, 0, 0:T], tmp[:, 1, 0:T], ALU.add), mixT_done)

            def residual(row):
                for t in range(TT):
                    for n in range(2):
                        xs = X[:, t, n * 512:(n + 1) * 512]
                        link(v.tensor_tensor(tmp[:, n, :], PB[2 + 2 * t + n][:, :], brow[:, row, n * 512:(n + 1) * 512],
                                             ALU.mult))
                        tell(v.tensor_tensor(xs, xs, tmp[:, n, :], ALU.add), x_done)

            def residual_plain(scale):
                for t in range(TT):
                    for n in range(2):
                        xs = X[:, t, n * 512:(n + 1) * 512]
                        tell(v.scalar_tensor_tensor(out=xs, in0=PB[2 + 2 * t + n][:, :], scalar=scale, in1=xs,
                                                    op0=ALU.mult, op1=ALU.add), x_done)

            dve.wait_ge(unit_done, UNIT[("wo", 3)] + 1)
            residual(0)
            norm(1)
            dve.wait_ge(xn_act, 2)
            for t in range(TT):
                link(v.tensor_tensor(XN[:, t, :], XN[:, t, :], brow[:, 1, :], ALU.mult))
                tell(v.tensor_tensor(XN[:, t, :], XN[:, t, :], brow[:, 2, :], ALU.add), h2_ready)
            evac_h(1, None, None)

            def top16(vals, idx, src):
                link(v.max(vals[:, 0:8], src))
                link(v.max_index(idx[:, 0:8], vals[:, 0:8], src))
                wk = work[:, 0:src.shape[1]]
                link(v.match_replace(out=wk, in_to_replace=vals[:, 0:8], in_values=src, imm_value=GONE))
                link(v.max(vals[:, 8:16], wk))
                link(v.max_index(idx[:, 8:16], vals[:, 8:16], wk))

            for t in range(TT):
                for h in range(16):
                    if h % 4 == 0:
                        dve.wait_ge(sc_done, 4 * t + h // 4 + 1)
                    top16(tv[:, h, :], ti[:, h, :], sco[:, t, h, :])
                link(v.tensor_copy(tif[:, :, :], ti[:, :, :]))
                tvv = tv[:, :, :].rearrange("p (h two) k -> p h two k", two=2)
                cv = cand.rearrange("p h (x y) -> p h x y", y=PK)
                link(v.tensor_tensor(cv, tvv[:, :, 0, :].unsqueeze(3).broadcast_to([P, PH, PK, PK]),
                                     tvv[:, :, 1, :].unsqueeze(2).broadcast_to([P, PH, PK, PK]), ALU.add))
                for h in range(PH):
                    top16(bv[:, h, :], bp[:, h * PK:(h + 1) * PK], cand[:, h, :])
                tell(v.tensor_tensor(gate[:, t, :, :], bv[:, :, :], bv[:, :, 0:1].broadcast_to([P, PH, PK]),
                                     ALU.subtract), gx_ready)
                link(v.tensor_scalar(bq[:, 0, :], bp[:, :], 4, None, ALU.logical_shift_right))
                link(v.tensor_scalar(bq[:, 1, :], bp[:, :], PK - 1, None, ALU.bitwise_and))
                link(v.tensor_copy(bqf[:, :, :], bq[:, :, :]))
                tifv = tif[:, :, :].rearrange("p (h two) k -> p h two k", two=2)
                for b in range(2):
                    link(v.tensor_tensor(oneh, bqf[:, b, :].unsqueeze(2).broadcast_to([P, NSLOT, PK]),
                                         iota16[:, :].unsqueeze(1).broadcast_to([P, NSLOT, PK]), ALU.is_equal))
                    o4 = oneh.rearrange("p (h k) x -> p h k x", h=PH)
                    link(v.tensor_tensor(o4, o4, tifv[:, :, b, :].unsqueeze(2).broadcast_to([P, PH, PK, PK]), ALU.mult))
                    link(v.tensor_reduce(ei[:, b, :], oneh, AX_X, ALU.add))
                link(v.scalar_tensor_tensor(out=ei[:, 0, :], in0=ei[:, 0, :], scalar=float(NKEYS), in1=ei[:, 1, :],
                                            op0=ALU.mult, op1=ALU.add))
                tell(v.tensor_copy(eidx[:, t, :], ei[:, 0, :]), route_ready)
                dve.wait_ge(ge_done, t + 1)
                link(v.tensor_reduce(gst[:, 0, :], gate[:, t, :, :], AX_X, ALU.add))
                link(v.reciprocal(gst[:, 1, :], gst[:, 0, :]))
                link(v.tensor_tensor(gate[:, t, :, :], gate[:, t, :, :],
                                     gst[:, 1, :].unsqueeze(2).broadcast_to([P, PH, PK]), ALU.mult))
            for t in range(TT):
                gt = gate[:, t, :, :].rearrange("p h k -> p (h k)")
                with dve.Fori(0, NSLOT // UVB) as i:
                    for g in range(2):
                        for j in range(4 * g, 4 * g + 4):
                            dve.wait_ge(uv_here[j], i * 16 + (t * (NSLOT // UVB) + 1) * 16)
                            v.tensor_tensor_reduce(out=uv[j][:, 0, :], in0=uv[j][:, 0, :], in1=XN[:, t, :], scale=1.0,
                                                   scalar=0.0, op0=ALU.mult, op1=ALU.add,
                                                   accum_out=dots[:, j:j + 1]).then_inc(dot_done, 1)
                        dve.wait_ge(gelu_done, i * 2 + (t * 2 * (NSLOT // UVB) + g + 1))
                        for j in range(4 * g, 4 * g + 4):
                            v.tensor_scalar(diag[:, j, :], ident[:, :], gl[:, j:j + 1], gt[:, bass.ds(i * UVB + j, 1)],
                                            ALU.mult, ALU.mult).then_inc(diag_done, 1)
            dve.wait_ge(diag_done, TT * NSLOT)
            count.n[diag_done.name] = TT * NSLOT
            dve.wait_ge(uv_used, TT * NSLOT + UVB)
            link(v.tensor_copy(stat[:, 10:11], stat[:, 9:10]))
            residual(3)

            def ffn(f):
                n, u0, a0 = N_FFN[f], ffn_base[f], FU * f
                norm(n)
                evac_h(n, gain(n), None)

                def one(j, i=None):
                    k = i * NS if i is not None else 0
                    dve.wait_ge(silu_done, k + (a0 + j + 1))
                    dve.wait_ge(unit_done, k + (u0 + j - 1))
                    v.tensor_tensor(act_a[:, j % 2, :], PB[j % 2][:, T:2 * T], act_gs[:, j % 2, :],
                                    ALU.mult).then_inc(a_done, 1)

                with dve.Fori(0, LOOPS) as i:
                    for j in range(NS):
                        one(j, i)
                for j in range(LOOPS * NS, FU):
                    one(j)
                dve.wait_ge(unit_done, u0 + FU)
                dve.wait_ge(a_done, a0 + FU + 2)
                count.n[a_done.name] = a0 + FU + 2
                residual_plain(0.5)

            ffn(0)
            norm(N_S5)
            evac_h(N_S5, gain(N_S5), None)
            dve.wait_ge(tab_ready, 2)
            for i in range(16):
                half, q = i // 8, i % 8
                if q % 2 == 0:
                    dve.wait_ge(bu_full, half * 4 + q // 2 + 1)
                else:
                    dve.wait_ge(unit_done, UNIT[("s5b", i // 2)] + 1)
                re = PB[2 + 2 * (i % 2)][:, :].rearrange("p (j s) -> p j s", j=4)
                im = PB[3 + 2 * (i % 2)][:, :].rearrange("p (j s) -> p j s", j=4)
                ec, es = Ec[:, 4 * q:4 * q + 4, :], Es[:, 4 * q:4 * q + 4, :]
                vr, vi, m0, m1 = (s5w[:, k, :, :] for k in (0, 1, 12, 13))
                link(v.tensor_tensor(vr, re, ec, ALU.mult))
                link(v.tensor_tensor(m0, im, es, ALU.mult))
                link(v.tensor_tensor(vi, im, ec, ALU.mult))
                tell(v.tensor_tensor(m1, re, es, ALU.mult), v_parts)
                link(v.tensor_tensor(vr, vr, m0, ALU.add))
                link(v.tensor_tensor(vi, vi, m1, ALU.subtract))
                if i >= 1:
                    dve.wait_ge(o_ready, i)
                for b, vv in ((0, vr), (1, vi)):
                    ww = s5w[:, 2 + b, :, :]
                    for j in range(4):
                        pair = 4 * q + j
                        init = 0.0 if half == 0 else s5p[:, 14 + b, pair:pair + 1]
                        ins = v.tensor_tensor_scan(ww[:, j, :], mag[:, pair:pair + 1].broadcast_to([P, HALF]), vv[:, j, :],
                                                   init, ALU.mult, ALU.add)
                        if b == 1 and j == 3:
                            tell(ins, w_ready)
                        elif j == 3:
                            link(ins)
                        else:
                            ins.then_inc(dve_link, 1)
                            count.up(dve_link)
                if half == 0:
                    wr, wi = s5w[:, 2, :, HALF - 1], s5w[:, 3, :, HALF - 1]
                    ps = slice(4 * q, 4 * q + 4)
                    link(v.tensor_tensor(t0[:, ps], wr, c128[:, ps], ALU.mult))
                    link(v.tensor_tensor(t1[:, ps], wi, s128[:, ps], ALU.mult))
                    link(v.tensor_tensor(s5p[:, 14, ps], t0[:, ps], t1[:, ps], ALU.subtract))
                    link(v.tensor_tensor(t0[:, ps], wr, s128[:, ps], ALU.mult))
                    link(v.tensor_tensor(t1[:, ps], wi, c128[:, ps], ALU.mult))
                    link(v.tensor_tensor(s5p[:, 15, ps], t0[:, ps], t1[:, ps], ALU.add))
                for k in ([i - 1] if i else []) + ([15] if i == 15 else []):
                    hk, qk = k // 8, k % 8
                    dve.wait_ge(y_full, k + 1)
                    ts = slice(hk * HALF, (hk + 1) * HALF)
                    tell(v.scalar_tensor_tensor(out=yT[:, qk, ts], in0=uT[:, qk, ts], scalar=col("d_skip")[:, qk:qk + 1],
                                                in1=PB[6 + k % 2][:, 0:HALF], op0=ALU.mult, op1=ALU.add), y_done)
            for c in range(DC):
                dve.wait_ge(sig_done, c + 1)
                tell(v.tensor_tensor(yT[:, c, :], yT[:, c, :], gT[:, c, :], ALU.mult), g2_done)
            dve.wait_ge(unit_done, UNIT[("s5out", 3)] + 1)
            residual_plain(1.0)
            ffn(1)
            ffn(2)

            norm(N_MOBA)
            evac_h(N_MOBA, gain(N_MOBA), None)
            for m in range(6):
                dve.wait_ge(unit_done, UNIT[("qkv", 2 * m + 1)] + 1)
                tell(v.tensor_copy(qkv[:, 1, 4 * m:4 * m + 4, :],
                                   PB[3 + 2 * (m % 2)][:, :].rearrange("p (h d) -> p h d", h=4)), mq_dve)
                if m == 3:
                    dve.wait_ge(mq_act, 4)
                    for t in range(TT):
                        z = qkv[:, t, 0:16, :]
                        link(v.tensor_tensor(msq[:, t, :, :], z, z, ALU.mult))
                        link(v.tensor_reduce(hstat[:, 0, 16 * t:16 * t + 16], msq[:, t, :, :], AX_X, ALU.add))
                    tell(v.tensor_scalar(hstat[:, 0, :], hstat[:, 0, :], 1.0 / MD, EPS, ALU.mult, ALU.add), hvar_ready)
            dve.wait_ge(hroot_ready, 2)
            newton(hstat[:, 2, :], hstat[:, 1, :], hstat[:, 0, :], hstat[:, 3, :], dve_link)
            for t in range(TT):
                z = qkv[:, t, 0:16, :]
                link(v.tensor_tensor(z, z, hstat[:, 2, 16 * t:16 * t + 16].unsqueeze(2).broadcast_to([P, 16, MD]),
                                     ALU.mult))
                zz = z.rearrange("p (a h) d -> p a h d", a=2)
                mg = rows[:, 3 * HD:3 * HD + 2 * MD].rearrange("p (a d) -> p a d", a=2)
                link(v.tensor_tensor(zz, zz, mg.unsqueeze(2).broadcast_to([P, 2, MH, MD]), ALU.mult))
                x1, x2 = z[:, :, 0:ROT], z[:, :, ROT:2 * ROT]
                cs = rope[:, t, 0, :].unsqueeze(1).broadcast_to([P, 16, ROT])
                sn = rope[:, t, 1, :].unsqueeze(1).broadcast_to([P, 16, ROT])
                r = [mrt[:, k, 0:16, :] for k in range(4)]
                link(v.tensor_tensor(r[0], x1, cs, ALU.mult))
                link(v.tensor_tensor(r[1], x2, sn, ALU.mult))
                link(v.tensor_tensor(r[2], x2, cs, ALU.mult))
                link(v.tensor_tensor(r[3], x1, sn, ALU.mult))
                link(v.tensor_tensor(x1, r[0], r[1], ALU.subtract))
                if t == 0:
                    link(v.tensor_tensor(x2, r[2], r[3], ALU.add))
                else:
                    tell(v.tensor_tensor(x2, r[2], r[3], ALU.add), qk_ready)
            for i in (1, 3, 5, 7):
                dve.wait_ge(mqT_full, i + 1)
                dst = (mqT if i < 4 else mkT)[:, 2 * (i % 4):2 * (i % 4) + 2, :]
                tell(v.tensor_copy(dst, PB[7][:, :].rearrange("p (h q) -> p h q", h=2)), mqT_dve)
            dve.wait_ge(causal_ready, 1)
            for t in range(TT):
                S = (t + 1) * P

                def mmask(g, dst, S=S, t=t):
                    src = PB[2 + g][:, :].rearrange("p (a s) -> p a s", a=2)
                    if t:
                        link(v.tensor_copy(mL[:, 2 * g:2 * g + 2, 0:P], src[:, :, 0:P]))
                    tell(v.tensor_tensor(mL[:, 2 * g:2 * g + 2, S - P:S], src[:, :, S - P:S],
                                         causal.unsqueeze(1).broadcast_to([P, 2, P]), ALU.add), L_done)

                softmax_head(2, t, mL, S, range(4), MD ** -0.5, mmask)
                for s in range(t + 1):
                    dve.wait_ge(pt_full, 6 + 2 * (t + s) + 2)
                    tell(v.tensor_copy(mPT[:, s, 1, :], PB[7][:, :]), pt_dve)
                dve.wait_ge(av_full, 3 + t)
                link(v.tensor_copy(moT[:, 0:4, t * P:(t + 1) * P], PB[0][:, :].rearrange("p (j q) -> p j q", j=4)))
                tell(v.tensor_copy(moT[:, 4:8, t * P:(t + 1) * P], PB[1][:, :].rearrange("p (j q) -> p j q", j=4)),
                     av_done)
            dve.wait_ge(unit_done, UNIT[("mo", 3)] + 1)
            residual_plain(1.0)
            ffn(3)

        @block.scalar
        def _(act):
            s = nc.scalar
            count = Count()

            def tell(ins, sm):
                ins.then_inc(sm, 1)
                act.wait_ge(sm, count.up(sm))

            act.dma_start(cols[:, :], a["cols"]).then_inc(small_here, 16)
            act.dma_start(X[:, :, :], a["x"].rearrange("(t p) d -> p t d", p=P)).then_inc(x_here, 16)
            act.dma_start(rows[:, :], a["rows"].partition_broadcast(P)).then_inc(small_here, 16)
            act.dma_start(rope[:, :, :, :], a["rope"]).then_inc(small_here, 16)
            act.dma_start(wgrp[:, :, :], a["w_grp"]).then_inc(small_here, 16)

            def norm(n):
                act.wait_ge(var_ready, n + 1)
                tell(s.activation(stat[:, 4:6], stat[:, 2:4], ACT.Sqrt), root_ready)
                act.wait_ge(rstd_ready, n + 1)
                tell(s.activation(XN[:, 0, :], X[:, 0, :], ACT.Copy, scale=stat[:, 6:7]), xn_act)

            def evac_h(n, scale, shift):
                for q in (1, 3):
                    act.wait_ge(tr_full, 4 * n + q + 1)
                    for j in range(2):
                        dc = 2 * q + j
                        src = PB[7][:, j * T:(j + 1) * T]
                        if scale is None:
                            ins = s.copy(hT[:, dc, :], src)
                        elif shift is None:
                            ins = s.activation(hT[:, dc, :], src, ACT.Copy, scale=scale[:, dc:dc + 1])
                        else:
                            ins = s.activation(hT[:, dc, :], src, ACT.Identity, bias=shift[:, dc:dc + 1],
                                               scale=scale[:, dc:dc + 1])
                        tell(ins, hT_act)

            def gain(n):
                return col("gain")[:, (n - 2) * DC:(n - 1) * DC]

            act.wait_ge(small_here, 16 * 4)
            tell(s.activation(s5p[:, 0, :], col("log_dt"), ACT.Exp), ang_ready)
            act.wait_ge(s5p_ready, 1)
            tell(s.activation(s5p[:, 1, :], s5p[:, 7, :], ACT.Exp), act_link)
            for b in range(4):
                m = 16 if b < 2 else 8
                tell(s.activation(base_t[:, b, :, 0:m], base_t[:, b, :, 0:m], ACT.Sin, scale=TWO_PI), act_link)
            tell(s.activation(s5p[:, 10:12, :], s5p[:, 10:12, :], ACT.Sin, scale=TWO_PI), trig_ready)
            norm(0)
            for i in range(8):
                act.wait_ge(brow_full, i + 1)
                tell(s.copy(brow[:, i // 2, (i % 2) * 512:(i % 2 + 1) * 512], PB[2 + i % 4][:, :]), brow_done)
            act.wait_ge(ada_ready, 3)
            evac_h(0, A1[:, :], ada[:, 0, :])
            act.wait_ge(unit_done, UNIT[("nat", 1)] + 1)
            for t in range(TT):
                tell(s.copy(zq[:, t, 0:NH, :], PB[2 + t][:, :].rearrange("p (h d) -> p h d", h=NH)), natq_out)
            act.wait_ge(hvar_ready, 1)
            tell(s.activation(hstat[:, 1, 0:24], hstat[:, 0, 0:24], ACT.Sqrt), hroot_ready)
            act.wait_ge(ident_ready, 4)

            def wait_chunk(name, i, c):
                if c == 0:
                    act.wait_ge(half_done, HALVES[(name, i)] + 1)
                else:
                    act.wait_ge(unit_done, UNIT[(name, i)] + 1)

            for c in range(6):
                wait_chunk("tz", c // 2, c % 2)
                dst = iqT[:, c, :] if c < 2 else pT[:, c - 2, 16:16 + T]
                tell(s.copy(dst, PB[c % 2][:, 0:T]), tz_done)
            for c in range(8):
                wait_chunk("zg", c // 2, c % 2)
                tell(s.activation(sg[:, c, :], PB[c % 2][:, 0:T], ACT.Sigmoid), tz_done)
            for p in range(6):
                act.wait_ge(qkT_full, p + 1)
                tell(s.copy(qkT[:, p, :], PB[6 + p % 2][:, 0:T]), qkT_done)

            def relus(t):
                S = (t + 1) * P
                act.wait_ge(idx_full, t + 1)
                if t:
                    act.wait_ge(mask_ready, t)
                for r in range(2):
                    src = PB[2 + 2 * t + r][:, :].rearrange("p (a s) -> p a s", a=2)[:, :, 0:S]
                    tell(s.activation(rel[:, 2 * r:2 * r + 2, 0:S], src, ACT.Relu, scale=HD ** -0.5), rel_done)

            relus(0)
            for c in range(8, 12):
                wait_chunk("zg", c // 2, c % 2)
                tell(s.activation(sg[:, c, :], PB[c % 2][:, 0:T], ACT.Sigmoid), tz_done)
            relus(1)
            for c in range(12, 16):
                wait_chunk("zg", c // 2, c % 2)
                tell(s.activation(sg[:, c, :], PB[c % 2][:, 0:T], ACT.Sigmoid), tz_done)
            for g in range(4):
                act.wait_ge(pg_full, g + 1)
                tell(s.activation(ypT[:, g, :], PB[g % 2][:, 0:T], ACT.Copy, scale=col("s_pool")[:, g:g + 1]), pg_done)

            def softmax(base, t, Lt, S, scale, pt, full):
                act.wait_ge(nm_ready, base + t + 1)
                for h in range(NH):
                    tell(s.activation(Lt[:, h, 0:S], Lt[:, h, 0:S], ACT.Exp, bias=rmax[:, 1, h:h + 1], scale=scale,
                                      accum_out=rmax[:, 2, h:h + 1]), exp_done if h == NH - 1 else act_link)
                for sk in range(t + 1):
                    act.wait_ge(pt_full, full + 2 * (t + sk) + 1)
                    tell(s.copy(pt[:, sk, 0, :], PB[6][:, :]), pt_act)

            for t in range(TT):
                softmax(0, t, L, (t + 1) * P, HD ** -0.5, PT, 0)
            norm(1)
            evac_h(1, None, None)
            act.dma_start(skd[:, :, :], a["skd"]).then_inc(sk_here, 16)
            for c in range(DC):
                wait_chunk("pq", c // 2, c % 2)
                tell(s.copy(pqT[:, c, :], PB[c % 2][:, 0:T]), pq_done)
            for t in range(TT):
                for hp in range(4):
                    act.wait_ge(sc_full, 4 * t + hp + 1)
                    tell(s.copy(sco[:, t, 4 * hp:4 * hp + 4, :], PB[2 + hp][:, :].rearrange("p (h k) -> p h k", h=4)),
                         sc_done)
            for t in range(TT):
                act.wait_ge(gx_ready, t + 1)
                tell(s.activation(gate[:, t, :, :], gate[:, t, :, :], ACT.Exp), ge_done)
            for t in range(TT):
                with act.Fori(0, NSLOT // UVB) as i:
                    for g in range(2):
                        act.wait_ge(dot_done, i * UVB + (t * NSLOT + 4 * g + 4))
                        s.activation(gl[:, 4 * g:4 * g + 4], dots[:, 4 * g:4 * g + 4], ACT.Gelu).then_inc(gelu_done, 1)

            def ffn(f):
                n, a0 = N_FFN[f], FU * f
                norm(n)
                evac_h(n, gain(n), None)

                def one(j, i=None):
                    k = i * NS if i is not None else 0
                    act.wait_ge(gu_done, k + (a0 + j + 1))
                    act.wait_ge(a_done, k + (a0 + j + 1))
                    s.activation(act_gs[:, j % 2, :], PB[j % 2][:, 0:T], ACT.Silu).then_inc(silu_done, 1)

                with act.Fori(0, LOOPS) as i:
                    for j in range(NS):
                        one(j, i)
                for j in range(LOOPS * NS, FU):
                    one(j)

            ffn(0)
            norm(N_S5)
            evac_h(N_S5, gain(N_S5), None)
            for c in range(DC):
                wait_chunk("s5in", c // 2, c % 2)
                tell(s.copy(uT[:, c, :], PB[c % 2][:, 0:T]), u_done)
            act.wait_ge(y_done, 16)
            tell(s.activation(gT, yT, ACT.Gelu_apprx_tanh), g_ready)
            for c in range(DC):
                wait_chunk("glu", c // 2, c % 2)
                tell(s.activation(yT[:, c, :], PB[c % 2][:, 0:T], ACT.Sigmoid), sig_done)
            ffn(1)
            ffn(2)
            norm(N_MOBA)
            evac_h(N_MOBA, gain(N_MOBA), None)
            for m in range(6):
                act.wait_ge(unit_done, UNIT[("qkv", 2 * m + 1)] + 1)
                tell(s.copy(qkv[:, 0, 4 * m:4 * m + 4, :], PB[2 + 2 * (m % 2)][:, :].rearrange("p (h d) -> p h d", h=4)),
                     mq_act)
            act.wait_ge(hvar_ready, 2)
            tell(s.activation(hstat[:, 1, :], hstat[:, 0, :], ACT.Sqrt), hroot_ready)
            for i in (0, 2, 4, 6):
                act.wait_ge(mqT_full, i + 1)
                dst = (mqT if i < 4 else mkT)[:, 2 * (i % 4):2 * (i % 4) + 2, :]
                tell(s.copy(dst, PB[6][:, :].rearrange("p (h q) -> p h q", h=2)), mqT_act)
            for t in range(TT):
                softmax(2, t, mL, (t + 1) * P, MD ** -0.5, mPT, 6)
            ffn(3)

        @block.gpsimd
        def _(pool):
            g = nc.gpsimd
            count = Count()

            def tell(ins, sm):
                ins.then_inc(sm, 1)
                pool.wait_ge(sm, count.up(sm))

            def link(ins):
                tell(ins, pool_link)

            link(g.memset(ident[:, :], 0.0))
            tell(g.affine_select(out=ident[:, :], in_=ident[:, :], pattern=[[-1, P]], compare_op=ALU.not_equal,
                                 fill=1.0, base=0, channel_multiplier=1), ident_ready)
            link(g.iota(iotai[:, 0:PK], pattern=[[1, PK]], base=0, channel_multiplier=0))
            tell(g.tensor_copy(iota16[:, :], iotai[:, 0:PK]), ident_ready)
            tell(g.iota(iotai[:, :], pattern=[[1, T]], base=1, channel_multiplier=0), ident_ready)
            tell(g.memset(pT[:, :, 0:16], 0.0), ident_ready)
            pool.wait_ge(tz_done, 6)
            src, dst = pT, pw0
            for st in range(4):
                d = 1 << st
                lo = 2 * d - 1
                link(g.tensor_tensor(dst[:, st:4, lo:PW], src[:, st:4, lo:PW], src[:, st:4, lo - d:PW - d], ALU.add))
                src, dst = dst, (pw1 if dst is pw0 else pw0)
            pool.wait_ge(rcnt_ready, 1)
            for w in range(4):
                sums = pw0 if w % 2 == 0 else pw1
                link(g.tensor_tensor(pw0[:, w, 0:T] if w % 2 else sums[:, w, 0:T], sums[:, w, 16:PW], rcnt[:, w, :],
                                     ALU.mult))
            tell(g.tensor_tensor(pw0[:, :, 0:T], pw0[:, :, 0:T], pT[:, :, 16:PW], ALU.subtract), mixp_ready)
            for t in range(TT):
                pool.wait_ge(route_ready, t + 1)
                with pool.Fori(0, NSLOT // UVB) as i:
                    for j in range(UVB):
                        pool.wait_ge(uv_used, i * UVB + (t * NSLOT + j + 1))
                        g.nop(nofuse=True)
                        g.tensor_copy(ibuf[:, j:j + 1], eidx[:, t, bass.ds(i * UVB + j, 1)]).then_inc(idx_copied, 1)
                        pool.wait_ge(idx_copied, i * UVB + (t * NSLOT + j + 1))
                        g.nop(nofuse=True)
                        g.indirect_dma_start(uv[j].rearrange("p a d -> p (a d)"), None, a["uv"],
                                             bass.IndirectOffsetOnAxis(ap=ibuf[:, j:j + 1], axis=0)).then_inc(uv_here[j], 16)
            pool.wait_ge(x_done, 8)
            pool.dma_start(cri, a["s5c"]).then_inc(c_here, 16)
            pool.wait_ge(s5p_ready, 2)
            cl, sl, ch, sh = (base_t[:, b, :, 0:m] for b, m in ((0, 16), (1, 16), (2, 8), (3, 8)))

            def lo_(x):
                return x.unsqueeze(2).broadcast_to([P, NPAIR, 8, 16])

            def hi_(x):
                return x.unsqueeze(3).broadcast_to([P, NPAIR, 8, 16])

            def grid(x):
                return x.rearrange("p n (h l) -> p n h l", l=16)

            link(g.tensor_tensor(grid(et0), hi_(ch), lo_(cl), ALU.mult))
            link(g.tensor_tensor(grid(et1), hi_(sh), lo_(sl), ALU.mult))
            link(g.tensor_tensor(Ec, et0, et1, ALU.subtract))
            link(g.tensor_tensor(grid(et0), hi_(sh), lo_(cl), ALU.mult))
            link(g.tensor_tensor(grid(et1), hi_(ch), lo_(sl), ALU.mult))
            link(g.tensor_tensor(Es, et0, et1, ALU.add))
            pool.wait_ge(c_here, 16)
            link(g.memset(CC.rearrange("p a b c -> p (a b c)"), 0.0))
            cre, cim = (s5p[:, b, :].unsqueeze(2).broadcast_to([P, NPAIR, SN]) for b in (8, 9))
            link(g.tensor_tensor(crt[:, 0, :, :], cri[:, 0, :, :], cre, ALU.mult))
            link(g.tensor_tensor(crt[:, 1, :, :], cri[:, 1, :, :], cim, ALU.mult))
            et0c = et0[:, 0:4, :].rearrange("p a b -> p (a b)").rearrange("p (n s) -> p n s", s=SN)
            et1c = et1[:, 0:4, :].rearrange("p a b -> p (a b)").rearrange("p (n s) -> p n s", s=SN)
            link(g.tensor_tensor(et0c, crt[:, 0, :, :], crt[:, 1, :, :], ALU.subtract))
            link(g.tensor_tensor(crt[:, 0, :, :], cri[:, 0, :, :], cim, ALU.mult))
            link(g.tensor_tensor(crt[:, 1, :, :], cri[:, 1, :, :], cre, ALU.mult))
            link(g.tensor_tensor(et1c, crt[:, 0, :, :], crt[:, 1, :, :], ALU.add))
            for b in range(2):
                pr, cs = slice(64 * b, 64 * b + 64), slice(SN * b, SN * (b + 1))
                link(g.tensor_copy(CC[pr, 0, :, cs], et0c[pr]))
                link(g.tensor_scalar(CC[pr, 1, :, cs], et0c[pr], -1.0, None, ALU.mult))
                tell(g.tensor_scalar(CC[pr, 2, :, cs], et1c[pr], -1.0, None, ALU.mult), tab_ready)
            for i in range(16):
                q = i % 8
                ec, es = Ec[:, 4 * q:4 * q + 4, :], Es[:, 4 * q:4 * q + 4, :]
                pool.wait_ge(w_ready, i + 1)
                if i >= 2:
                    pool.wait_ge(y_full, i - 1)
                wr, wi = s5w[:, 2, :, :], s5w[:, 3, :, :]
                o = [s5w[:, 4 + 4 * (i % 2) + k, :, :] for k in range(4)]
                link(g.tensor_tensor(o[0], wr, ec, ALU.mult))
                link(g.tensor_tensor(o[1], wi, es, ALU.mult))
                link(g.tensor_tensor(o[2], wr, es, ALU.mult))
                tell(g.tensor_tensor(o[3], wi, ec, ALU.mult), o_ready)
            pool.wait_ge(x_done, 16)
            link(g.memset(causal, 0.0))
            tell(g.affine_select(out=causal, in_=causal, pattern=[[-1, P]], compare_op=ALU.is_ge, fill=NEG, base=0,
                                 channel_multiplier=1), causal_ready)


def layouts(i):
    f = {k: np.asarray(v, np.float32) if np.asarray(v).dtype == np.float32 else np.asarray(v) for k, v in i.items()}

    def chunked(w, per):
        k, n = w.shape
        b = w.reshape(k // P, P, n // P, P).transpose(2, 1, 0, 3)
        return b.reshape(n // P // per, per, P, k // P, P).transpose(0, 2, 1, 3, 4).reshape(n // P // per, P, -1)

    def rows_of(w, per):
        k, n = w.shape
        return w.reshape(k // P // per, per, P, n).transpose(0, 2, 1, 3).reshape(k // P // per, P, -1)

    def colv(v):
        return v.reshape(-1, P).T

    w_in = f["w_in"][0]
    q, k, v, iq, ik, iw, zp, zg = np.split(w_in, [512, 576, 640, 896, 960, 964, 1476], axis=1)
    o = {}
    o["ada"] = chunked(f["w_ada"][0], 3)
    o["nat"] = rows_of(np.concatenate([q, k, ik, v, iw], 1), 4)
    o["tz"] = chunked(np.concatenate([iq, zp], 1), 2)
    o["zg"] = chunked(zg, 2)
    o["up"] = chunked(np.concatenate([f["w_up_attn"][0], f["w_up_pool"][0]], 0), 2)
    o["wo"] = rows_of(f["w_out"][0], 2)
    o["pq"] = chunked(f["w_peer_q"][0], 2)
    ff = []
    for layer in range(2):
        for b in range(2):
            g = chunked(f["ffn_w_gate_2"][layer, b], 1)
            u = chunked(f["ffn_w_up_2"][layer, b], 1)
            d = rows_of(f["ffn_w_down_2"][layer, b], 1)
            ff.append(np.concatenate([g, u, d], 2))
    o["ffn"] = np.concatenate(ff, 0)
    o["s5in"] = chunked(f["s5_w_in_2"][0], 2)
    sb_ = np.zeros((2, 8, 4, 2, SN, 4, 2, SP_), np.float32)
    for b, name in enumerate(("s5_b_re_2", "s5_b_im_2")):
        bb = f[name][0].reshape(8, 4, 2, SP_, SN)
        for j in range(4):
            for g in range(2):
                sb_[b, :, j, g, :, j, g, :] = bb[:, j, g].transpose(0, 2, 1)
    sb_ = sb_.reshape(2, 4, 2, P, 4 * P).transpose(1, 3, 2, 0, 4).reshape(4, P, -1)
    o["s5b"] = np.concatenate([sb_, sb_], 0)
    o["s5c"] = np.stack([f[n][0].reshape(NPAIR, 2, SN, SP_).transpose(1, 3, 0, 2).reshape(P, NPAIR, SN)
                         for n in ("s5_c_re_2", "s5_c_im_2")], 1)
    o["glu"] = chunked(f["s5_w_glu_2"][0], 2)
    o["s5out"] = rows_of(f["s5_w_out_2"][0], 2)
    qkv = f["moba_w_qkv_2"][0]
    o["qkv"] = np.stack([rows_of(qkv[:, 512 * m:512 * (m + 1)], 4) for m in range(6)]).reshape(12, P, -1)
    o["mo"] = rows_of(f["moba_w_out_2"][0], 2)

    def pairs(v):
        return v.reshape(NPAIR, P).T

    fn, mn = f["ffn_norm_2"], f["mix_norm_2"]
    o["cols"] = np.concatenate([
        colv(f["c"][0]), colv(f["b_ada"][0]), colv(f["g_norm1"][0]), colv(f["g_norm2"][0]),
        colv(fn[0, 0]), colv(mn[0]), colv(fn[0, 1]), colv(fn[1, 0]), colv(mn[1]), colv(fn[1, 1]),
        colv(f["s_pool"][0].reshape(-1)), colv(f["s5_d_2"][0]),
        pairs(f["s5_a_re_2"][0]), pairs(f["s5_a_im_2"][0]),
        pairs(np.broadcast_to(f["s5_log_dt_2"][0][:, None], (SG, SP_)))], 1)
    o["rows"] = np.concatenate([f["g_q"][0], f["g_k"][0], f["g_ik"][0],
                                f["moba_q_norm_2"][0], f["moba_k_norm_2"][0]])
    inv = np.float32(500000.0) ** (-np.arange(0, 2 * ROT, 2, dtype=np.float32) / np.float32(2 * ROT))
    ang = np.arange(T, dtype=np.float32)[:, None] * inv[None, :]
    o["rope"] = np.stack([np.cos(ang), np.sin(ang)], 1).astype(np.float32).reshape(TT, P, 2, ROT).transpose(1, 0, 2, 3)
    o["w_grp"] = f["w_pool_grp"][0].transpose(1, 0, 2)
    sk = f["peer_subkeys"][0]
    skd = np.zeros((2, HD, PH, 2, NKEYS), np.float32)
    for b in range(2):
        skd[b, :, :, b, :] = sk[:, b].transpose(2, 0, 1)
    o["skd"] = skd.reshape(P, PH, 2 * NKEYS)
    o["uv"] = np.concatenate([f["peer_u"][0], f["peer_v"][0]], 1)
    o["x"] = f["x"][0]
    return {n: np.ascontiguousarray(x) for n, x in o.items()}


def program(nc, arrays):
    args = {n: nc.dram_tensor(f"in_{n}", x.shape, mybir.dt.from_np(x.dtype), kind="ExternalInput").ap()
            for n, x in arrays.items()}
    out = nc.dram_tensor("out_0", (T, D), F32, kind="ExternalOutput").ap()
    build(nc, args, out)


def kernel(**inputs):
    import concourse.bacc as bacc
    from concourse.bass_utils import run_bass_kernel_spmd

    arrays = layouts(inputs)
    nc = bacc.Bacc("TRN2", target_bir_lowering=False, num_devices=1)
    program(nc, arrays)
    r = run_bass_kernel_spmd(nc, [{f"in_{n}": x for n, x in arrays.items()}], core_ids=[0])
    return r.results[0]["out_0"].reshape(1, T, D)
```

```python
from contextlib import ExitStack

import numpy as np

import concourse.bass as bass
from concourse import mybir

F32 = mybir.dt.float32
F32R = mybir.dt.float32r
U32 = mybir.dt.uint32
ALU = mybir.AluOpType
ACT = mybir.ActivationFunctionType
AX_X = mybir.AxisListType.X

P = 128
D = 1024
DC = D // P
T = 256
TT = T // P
EPS = 1e-6
NEG = -1e30
GONE = -3e38

NH, HD = 8, 64
IH = 4
TOPK = min(256, T // 4)
NATQ = NH * HD
NATW = NATQ + 3 * HD + IH
PH, PK, NKEYS = 8, 16, 128
NSLOT = PH * PK
UVB = 8
ROUTE_ROUNDS = 8
EXP_ROUND = 6
FF = 2816
FU = FF // P
SG, SP_, SN = 64, 64, 16
NPAIR = SG // 2
HALF = T // 2
MH, MD = 8, 128
ROT = MD // 8

NS = 4
SLOT = 3072
ADW = 768
TWO_PI = 6.283185
MAGIC = 12582912.0


def unit_plan():
    plan = []

    def add(name, n, words):
        plan.extend((name, i, words) for i in range(n))

    add("ada", 16, DC // 2 * ADW)
    add("nat", 2, DC // 2 * NATW)
    add("tz", 3, 2 * DC * P)
    add("zg", 8, 2 * DC * P)
    add("up", 4, 2 * DC * P)
    add("wo", 4, 2 * D)
    add("pq", 4, 2 * DC * P)
    add("ffn0", FU, SLOT)
    add("s5in", 4, 2 * DC * P)
    add("s5b", 8, 4 * 4 * P)
    add("glu", 4, 2 * DC * P)
    add("s5out", 4, 2 * D)
    add("ffn1", FU, SLOT)
    add("ffn2", FU, SLOT)
    add("qkv", 12, 4 * 512)
    add("mo", 4, 2 * D)
    add("ffn3", FU, SLOT)
    return plan


PLAN = unit_plan()
UNIT = {(name, i): u for u, (name, i, _) in enumerate(PLAN)}
TWO_CHUNKS = ("tz", "zg", "up", "pq", "s5in", "glu")
HALVES = {}
for _name, _i, _ in PLAN:
    if _name in TWO_CHUNKS:
        HALVES[(_name, _i)] = len(HALVES)

SPLIT = {}
for _name, _i, _ in PLAN:
    if _name in ("s5in", "qkv"):
        SPLIT[(_name, _i)] = len(SPLIT)

COLS = {}
_at = 0
for _name, _n in (("c", DC), ("b_ada", 6 * DC), ("g1", DC), ("g2", DC), ("gain", 6 * DC), ("s_pool", 4),
                  ("d_skip", DC), ("a_re", NPAIR), ("a_im", NPAIR), ("log_dt", NPAIR)):
    COLS[_name] = (_at, _at + _n)
    _at += _n
NCOL = _at


class Count:

    def __init__(self):
        self.n = {}

    def up(self, sem):
        self.n[sem.name] = self.n.get(sem.name, 0) + 1
        return self.n[sem.name]


def build(nc, a, out):
    ctx = ExitStack()
    with ctx:
        def sb(name, shape, dt=F32):
            return ctx.enter_context(nc.sbuf_tensor(name, shape, dt))

        def sem(name):
            return ctx.enter_context(nc.semaphore(name))

        ring = sb("ring", [P, NS, SLOT])
        X = sb("X", [P, TT, D])
        XN = sb("XN", [P, TT, D])
        hT_at = nc.sbuf_base
        hT = sb("hT", [P, DC, T])
        ident = sb("ident", [P, P])
        zeros = sb("zeros", [P, P])
        ones = sb("ones", [P, 2])
        cols = sb("cols", [P, NCOL])
        rows = sb("rows", [P, 3 * HD + 2 * MD])
        rope = sb("rope", [P, TT, 2, ROT])
        ada = sb("ada", [P, 6, DC])
        A1 = sb("A1", [P, DC])
        A2 = sb("A2", [P, DC])
        stat = sb("stat", [P, 16])
        hstat = sb("hstat", [P, 4, 32])
        act_gs = sb("act_gs", [P, 2, T])
        act_a = sb("act_a", [P, T])
        s5p = sb("s5p", [P, 16, NPAIR])
        base_lo = sb("base_lo", [P, 2, NPAIR, 16])
        base_hi = sb("base_hi", [P, 2, NPAIR, 8])
        base = [base_lo[:, 0, :, :], base_lo[:, 1, :, :], base_hi[:, 0, :, :], base_hi[:, 1, :, :]]
        arena_at = nc.sbuf_base
        arena = sb("arena", [P, 28672])

        def split_at(name, shape, at):
            return nc.alloc_sbuf_tensor_at(name, shape, F32R, offset=at)

        h_hi = split_at("h_hi", [P, DC, T], hT_at)
        h_lo = split_at("h_lo", [P, DC, T], arena_at + 4 * 14336)
        gu_hi = split_at("gu_hi", [P, 2, 2 * D], arena_at + 4 * 16384)
        gu_lo = split_at("gu_lo", [P, 2, 2 * D], arena_at + 4 * 20480)
        dn_hi = split_at("dn_hi", [P, 2, D], arena_at + 4 * 24576)
        dn_lo = split_at("dn_lo", [P, 2, D], arena_at + 4 * 26624)
        a_hi = sb("a_hi", [P, 2, T], F32R)
        a_lo = sb("a_lo", [P, 2, T], F32R)

        def part(at, *shape):
            n = int(np.prod(shape))
            v = arena[:, at:at + n]
            if len(shape) == 2:
                v = v.rearrange("p (a b) -> p a b", b=shape[1])
            if len(shape) == 3:
                v = v.rearrange("p (a b c) -> p a b c", b=shape[1], c=shape[2])
            return v

        brow = part(0, 4, D)
        zq = part(4096, TT, 12, HD)
        sq = part(5632, TT, 12, HD)
        vn = part(7168, TT, HD)
        iw = part(7296, TT, IH)
        qkT = part(7304, 6, T)
        iqT = part(8840, 2, T)
        PW = 16 + T
        pT = part(9352, 4, PW)
        pw0 = part(10440, 4, PW)
        pw1 = part(11528, 4, PW)
        rel = part(12616, 4, T)
        score = part(13640, 2, T)
        maskb = part(14152, TT, T)
        sg = part(14664, 16, T)
        L = part(18760, NH, T)
        PT = part(20808, 2, 2, 4 * P)
        yat = part(22856, 4, T)
        ypT = part(23880, 4, T)
        mixT = part(24904, DC, T)
        tmp = part(26952, 2, 512)
        rcnt = part(26952, 4, T)
        wgrp = part(27976, 4, P)
        accA = part(18432, 6 * D)
        skd = part(4096, PH, 2 * NKEYS)
        pqT = part(6144, DC, T)
        sco = part(8192, TT, 16, NKEYS)
        cand = part(12288, PH, PK * PK)
        oneh = part(14336, NSLOT, PK)
        uv = [part(16384 + 2048 * j, 2, D) for j in range(6)] + [part(4096 + 2048 * j, 2, D) for j in range(2)]
        Ec = part(0, NPAIR, HALF)
        Es = part(4096, NPAIR, HALF)
        et0 = part(8192, NPAIR // 2, HALF)
        et1 = part(10240, NPAIR // 2, HALF)
        cri = part(8192, 2, NPAIR, SN)
        crt = part(9216, 2, NPAIR, SN)
        cp_re = part(10240, NPAIR, SN)
        cp_im = part(10752, NPAIR, SN)
        CC = part(11264, 3, NPAIR, 2 * SN)
        gT = part(8192, DC, T)
        s5w = part(16384, 16, 4, HALF)
        W_AT = (2, 14)
        uT = part(24576, DC, T)
        yT = part(26624, DC, T)
        qkv = part(0, TT, 24, MD)
        msq = part(6144, 2, 16, MD)
        mrt = part(10240, 4, TT * 16, ROT)
        mqT = part(12288, MH, T)
        mkT = part(14336, MH, T)
        mL = part(16384, MH, T)
        mPT = part(18432, 2, 2, 4 * P)
        moT = part(20480, MH, T)
        causal = part(24576, P)

        hflat = hT[:, :, :].rearrange("p a b -> p (a b)")

        def hpart(at, a_, b_):
            return hflat[:, at:at + a_ * b_].rearrange("p (a b) -> p a b", b=b_)

        tv = hpart(0, 16, PK)
        ti = hpart(256, 16, PK).bitcast(U32)
        tif = hpart(512, 16, PK)
        work = hflat[:, 768:1024]
        bv = hpart(1024, PH, PK)
        bp = hflat[:, 1152:1280].bitcast(U32)
        bq = hpart(1280, 2, NSLOT).bitcast(U32)
        bqf = hpart(1536, 2, NSLOT)
        ei = hpart(1792, 2, NSLOT)
        diag = part(0, UVB, P)
        eidx = sb("eidx", [P, TT, NSLOT], U32)
        gate = sb("gate", [P, TT, PH, PK])
        gst = sb("gst", [P, 2, PH])
        iota16 = sb("iota16", [P, PK])
        iotai = part(14664, T).bitcast(U32)
        ibuf = sb("ibuf", [P, UVB], U32)
        dots = sb("dots", [P, UVB])
        gl = sb("gl", [P, UVB])
        top8 = sb("top8", [P, 8])
        rmax = sb("rmax", [P, 4, NH])

        PB = [ctx.enter_context(nc.psum_tensor(f"PB{b}", [P, 512], F32)) for b in range(8)]

        x_here = sem("x_here")
        small_here = sem("small_here")
        sk_here = sem("sk_here")
        c_here = sem("c_here")
        w_here = [sem(f"w_here{s}") for s in range(NS)]
        unit_done = sem("unit_done")
        half_done = sem("half_done")
        ident_ready = sem("ident_ready")
        dve_link, act_link, pool_link = sem("dve_link"), sem("act_link"), sem("pool_link")
        ada_full, ada_ready = sem("ada_full"), sem("ada_ready")
        brow_full, brow_done = sem("brow_full"), sem("brow_done")
        var_ready, root_ready, rstd_ready = sem("var_ready"), sem("root_ready"), sem("rstd_ready")
        xn_act, xn_dve, h2_ready = sem("xn_act"), sem("xn_dve"), sem("h2_ready")
        tr_full, hT_dve, hT_act = sem("tr_full"), sem("hT_dve"), sem("hT_act")
        natq_out, nat_out = sem("natq_out"), sem("nat_out")
        hvar_ready, hroot_ready, qk_ready = sem("hvar_ready"), sem("hroot_ready"), sem("qk_ready")
        tz_done = sem("tz_done")
        qkT_full, qkT_done = sem("qkT_full"), sem("qkT_done")
        idx_full, rel_done, mask_ready = sem("idx_full"), sem("rel_done"), sem("mask_ready")
        lg_full, L_done, nm_ready, exp_done, p_ready = (sem("lg_full"), sem("L_done"), sem("nm_ready"),
                                                        sem("exp_done"), sem("p_ready"))
        pt_full, pt_act, pt_dve = sem("pt_full"), sem("pt_act"), sem("pt_dve")
        av_full, av_done = sem("av_full"), sem("av_done")
        mixp_ready, pg_full, pg_done = sem("mixp_ready"), sem("pg_full"), sem("pg_done")
        rcnt_ready = sem("rcnt_ready")
        mixT_done = sem("mixT_done")
        x_done = sem("x_done")
        pq_done = sem("pq_done")
        sc_full, sc_done = sem("sc_full"), sem("sc_done")
        gx_ready, ge_done, route_ready = sem("gx_ready"), sem("ge_done"), sem("route_ready")
        idx_copied = sem("idx_copied")
        uv_here = [sem(f"uv_here{j}") for j in range(UVB)]
        dot_done, gelu_done, diag_done, uv_used = sem("dot_done"), sem("gelu_done"), sem("diag_done"), sem("uv_used")
        gu_done, silu_done, a_done = sem("gu_done"), sem("silu_done"), sem("a_done")
        pw_hi_done, pw_lo_done = sem("pw_hi_done"), sem("pw_lo_done")
        gu_hi_done, gu_lo_done, dn_hi_done, dn_lo_done = (sem("gu_hi_done"), sem("gu_lo_done"), sem("dn_hi_done"),
                                                          sem("dn_lo_done"))
        prod_done, a_hi_done = sem("prod_done"), sem("a_hi_done")
        hs_dve = sem("hs_dve")
        ang_ready, trig_ready, s5p_ready = sem("ang_ready"), sem("trig_ready"), sem("s5p_ready")
        tab_ready = sem("tab_ready")
        u_done, bu_full, v_parts = sem("u_done"), sem("bu_full"), sem("v_parts")
        w_ready, o_ready, y_full, y_done = sem("w_ready"), sem("o_ready"), sem("y_full"), sem("y_done")
        g_ready, sig_done, g2_done = sem("g_ready"), sem("sig_done"), sem("g2_done")
        mq_act, mq_dve = sem("mq_act"), sem("mq_dve")
        causal_ready = sem("causal_ready")
        mqT_full, mqT_act, mqT_dve = sem("mqT_full"), sem("mqT_act"), sem("mqT_dve")
        stored = sem("stored")

        def col(name):
            return cols[:, COLS[name][0]:COLS[name][1]]

        def w_chunk(u, c, k, kn=DC):
            o = (c * kn + k) * P
            return ring[:, u % NS, o:o + P]

        ffn_base = [UNIT[(f"ffn{f}", 0)] for f in range(4)]
        LOOPS = FU // NS
        N_FFN, N_S5, N_MOBA = (2, 4, 5, 7), 3, 6
        SPLIT_NORM = 2

        block = ctx.enter_context(nc.Block())

        @block.sync
        def _(sp):
            def load(name, n):
                for i in range(n):
                    u = UNIT[(name, i)]
                    words = PLAN[u][2]
                    if u >= NS:
                        sp.wait_ge(unit_done, u - NS + 1)
                    sp.dma_start(ring[:, u % NS, 0:words], a[name][i]).then_inc(w_here[u % NS], 16)

            def load_ffn(f):
                w = a["ffn"].rearrange("u p w -> (u p) w")
                u0 = ffn_base[f]

                def one(j, row):
                    sp.dma_start(ring[:, (u0 + j) % NS, :], w[bass.ds(row, P), :]).then_inc(
                        w_here[(u0 + j) % NS], 16)

                with sp.Fori(0, LOOPS) as i:
                    for j in range(NS):
                        sp.wait_ge(unit_done, i * NS + (u0 + j - NS + 1))
                        one(j, i * (NS * P) + (f * FU + j) * P)
                for j in range(LOOPS * NS, FU):
                    sp.wait_ge(unit_done, u0 + j - NS + 1)
                    one(j, (f * FU + j) * P)

            load("ada", 16)
            load("nat", 2)
            load("tz", 3)
            load("zg", 8)
            load("up", 4)
            load("wo", 4)
            load("pq", 4)
            load_ffn(0)
            load("s5in", 4)
            load("s5b", 8)
            load("glu", 4)
            load("s5out", 4)
            load_ffn(1)
            load_ffn(2)
            load("qkv", 12)
            load("mo", 4)
            load_ffn(3)
            sp.wait_ge(x_done, 4 * 8)
            sp.dma_start(out.rearrange("(t p) d -> p t d", p=P), X[:, :, :]).then_inc(stored, 16)
            sp.wait_ge(stored, 16)

        @block.tensor
        def _(pe):
            def here(u):
                pe.wait_ge(w_here[u % NS], 16 * (u // NS + 1))

            def h_ready(n):
                if n < SPLIT_NORM:
                    pe.wait_ge(hT_dve, 4 * (n + 1))
                else:
                    pe.wait_ge(hs_dve, 12 * (n - SPLIT_NORM + 1))
                pe.wait_ge(hT_act, 4 * (n + 1))

            def transposes(n):
                if n == 1:
                    pe.wait_ge(h2_ready, TT)
                else:
                    pe.wait_ge(xn_act, n + 1)
                    pe.wait_ge(xn_dve, n + 1)
                for q in range(4):
                    if q >= 2 and n >= SPLIT_NORM:
                        pe.wait_ge(hs_dve, 12 * (n - SPLIT_NORM) + (4, 6)[q - 2])
                    elif q == 2:
                        pe.wait_ge(hT_dve, 4 * n + 2)
                    elif q == 3:
                        pe.wait_ge(hT_act, 4 * n + 2)
                    for j in range(2):
                        for t in range(TT):
                            dc = 2 * q + j
                            mm = pe.transpose(PB[6 + q % 2][:, j * T + t * P:j * T + (t + 1) * P],
                                              XN[:, t, dc * P:(dc + 1) * P], ident[:, :])
                    mm.then_inc(tr_full, 1)

            def chunks(name, n, src, banks_free):
                for i in range(n):
                    u = UNIT[(name, i)]
                    here(u)
                    for c in range(2):
                        banks_free(2 * i + c)
                        for k in range(DC):
                            mm = pe.matmul(PB[c][:, 0:T], lhsT=w_chunk(u, c, k), rhs=src[:, k, :],
                                           start=(k == 0), stop=(k == DC - 1))
                        mm.then_inc(half_done if c == 0 else unit_done, 1)

            products = ((gu_hi, h_hi), (gu_hi, h_lo), (gu_lo, h_hi))

            def split_chunks(name, n, banks_free):
                for i in range(n):
                    w_part = SPLIT[(name, i)]
                    pe.wait_ge(pw_lo_done, w_part + 1)
                    for c in range(2):
                        banks_free(2 * i + c)
                        for k in range(DC):
                            o = (c * DC + k) * P
                            for m, (w, h) in enumerate(products):
                                mm = pe.matmul(PB[c][:, 0:T], lhsT=w[:, w_part % 2, o:o + P], rhs=h[:, k, :],
                                               start=(k == 0 and m == 0), stop=(k == DC - 1 and m == 2))
                        mm.then_inc(half_done if c == 0 else unit_done, 1)

            def natural(name, src):
                for i in range(4):
                    u = UNIT[(name, i)]
                    here(u)
                    for kk in range(2):
                        k = 2 * i + kk
                        for t in range(TT):
                            for n in range(2):
                                mm = pe.matmul(PB[2 + 2 * t + n][:, :], lhsT=src[:, k, t * P:(t + 1) * P],
                                               rhs=ring[:, u % NS, kk * D + n * 512:kk * D + (n + 1) * 512],
                                               start=(k == 0), stop=(k == DC - 1))
                    mm.then_inc(unit_done, 1)

            def free01(done, before):
                def wait(c):
                    if before + c >= 2:
                        pe.wait_ge(done, before + c - 1)
                return wait

            for r in range(6 * D // ADW):
                pe.wait_ge(unit_done, 2 * r + 2)
                for j in range(r * (ADW // P), (r + 1) * (ADW // P)):
                    mm = pe.matmul(PB[6][:, j:j + 1], lhsT=accA[:, j * P:(j + 1) * P], rhs=ones[:, 0:1],
                                   start=True, stop=True)
            mm.then_inc(ada_full, 1)
            pe.wait_ge(ident_ready, 1)
            pe.wait_ge(ada_ready, 3)
            for i in range(8):
                if i >= 4:
                    pe.wait_ge(brow_done, i - 3)
                src = (ada[:, 2, :], A2[:, :], ada[:, 3, :], ada[:, 5, :])[i // 2]
                for j in range(4):
                    c = 4 * (i % 2) + j
                    mm = pe.matmul(PB[2 + i % 4][:, j * P:(j + 1) * P], lhsT=src[:, c:c + 1].broadcast_to([P, P]),
                                   rhs=ident[:, :], start=True, stop=True)
                mm.then_inc(brow_full, 1)
            transposes(0)
            h_ready(0)
            pe.wait_ge(brow_done, 8)
            for i in range(2):
                u = UNIT[("nat", i)]
                here(u)
                for kk in range(4):
                    k = 4 * i + kk
                    for t in range(TT):
                        for b, lo, hi in ((2, 0, NATQ), (4, NATQ, NATW)):
                            mm = pe.matmul(PB[b + t][:, 0:hi - lo], lhsT=hT[:, k, t * P:(t + 1) * P],
                                           rhs=ring[:, u % NS, kk * NATW + lo:kk * NATW + hi],
                                           start=(k == 0), stop=(k == DC - 1))
                mm.then_inc(unit_done, 1)
            chunks("tz", 3, hT, free01(tz_done, 0))

            def gates(i0, i1):
                for i in range(i0, i1):
                    u = UNIT[("zg", i)]
                    here(u)
                    for c in range(2):
                        pe.wait_ge(tz_done, 6 + 2 * i + c - 1)
                        for k in range(DC):
                            mm = pe.matmul(PB[c][:, 0:T], lhsT=w_chunk(u, c, k), rhs=hT[:, k, :],
                                           start=(k == 0), stop=(k == DC - 1))
                        mm.then_inc(half_done if c == 0 else unit_done, 1)

            gates(0, 4)
            pe.wait_ge(qk_ready, 1)
            for p in range(6):
                if p >= 2:
                    pe.wait_ge(qkT_done, p - 1)
                for t in range(TT):
                    mm = pe.transpose(PB[6 + p % 2][:, t * P:(t + 1) * P],
                                      zq[:, t, 2 * p:2 * p + 2, :].rearrange("p a b -> p (a b)"), ident[:, :])
                mm.then_inc(qkT_full, 1)
            pe.wait_ge(qkT_done, 6)
            pe.wait_ge(tz_done, 2)
            pe.wait_ge(nat_out, 2)
            pe.wait_ge(natq_out, 2)
            for t in range(TT):
                S = (t + 1) * P
                for h in range(IH):
                    r, o = h % 2, (h // 2) * T
                    mm = pe.matmul(PB[2 + 2 * t + r][:, o:o + S], lhsT=iqT[r * HD:(r + 1) * HD, h // 2, t * P:(t + 1) * P],
                                   rhs=qkT[r * HD:(r + 1) * HD, 5, 0:S], start=True, stop=True)
                mm.then_inc(idx_full, 1)
            gates(4, 8)
            pe.wait_ge(mixp_ready, 1)
            for g in range(4):
                if g < 2:
                    pe.wait_ge(tz_done, 21 + g)
                else:
                    pe.wait_ge(pg_done, g - 1)
                pe.matmul(PB[g % 2][:, 0:T], lhsT=wgrp[:, g, :], rhs=pw0[:, g, 0:T],
                          start=True, stop=True).then_inc(pg_full, 1)
            for t in range(TT):
                S = (t + 1) * P
                pe.wait_ge(rel_done, 4)
                if t:
                    pe.wait_ge(L_done, 4)
                for h in range(NH):
                    r, j = h % 2, h // 2
                    mm = pe.matmul(PB[2 + r + 2 * (j // 2)][:, (j % 2) * T:(j % 2) * T + S],
                                   lhsT=qkT[r * HD:(r + 1) * HD, j, t * P:(t + 1) * P],
                                   rhs=qkT[r * HD:(r + 1) * HD, 4, 0:S], start=True, stop=True)
                mm.then_inc(lg_full, 1)
                pe.wait_ge(p_ready, t + 1)
                for s in range(t + 1):
                    if t + s > 0:
                        pe.wait_ge(pt_act, t + s)
                        pe.wait_ge(pt_dve, t + s)
                    for r in range(2):
                        for j in range(4):
                            mm = pe.transpose(PB[6 + r][:, j * P:(j + 1) * P], L[:, 2 * j + r, s * P:(s + 1) * P],
                                              ident[:, :])
                        mm.then_inc(pt_full, 1)
                if t == 0:
                    pe.wait_ge(pg_done, 4)
                pe.wait_ge(pt_act, t + t + 1)
                pe.wait_ge(pt_dve, t + t + 1)
                for s in range(t + 1):
                    for r in range(2):
                        mm = pe.matmul(PB[t][r * HD:(r + 1) * HD, :], lhsT=vn[:, s, :], rhs=PT[:, s, r, :],
                                       start=(s == 0), stop=(s == t), skip_group_check=True)
                mm.then_inc(av_full, 1)
            pe.wait_ge(av_done, 2)
            for i in range(4):
                u = UNIT[("up", i)]
                here(u)
                for c in range(2):
                    dc = 2 * i + c
                    if dc >= 2:
                        pe.wait_ge(mixT_done, dc - 1)
                    for b, src in enumerate((yat, ypT)):
                        for k in range(4):
                            mm = pe.matmul(PB[c][:, b * T:(b + 1) * T], lhsT=w_chunk(u, c, 4 * b + k),
                                           rhs=src[:, k, :], start=(k == 0), stop=(k == 3))
                    mm.then_inc(half_done if c == 0 else unit_done, 1)
            pe.wait_ge(mixT_done, DC)
            natural("wo", mixT)
            transposes(1)
            h_ready(1)
            chunks("pq", 4, hT, lambda c: pe.wait_ge(pq_done, c - 1) if c >= 2 else None)
            pe.wait_ge(pq_done, 8)
            pe.wait_ge(sk_here, 16)
            pe.wait_ge(x_done, 4)
            for t in range(TT):
                for hp in range(4):
                    if t:
                        pe.wait_ge(sc_done, hp + 1)
                    for j in range(2):
                        h = 2 * hp + j
                        mm = pe.matmul(PB[2 + hp][:, j * 256:(j + 1) * 256], lhsT=pqT[:, h, t * P:(t + 1) * P],
                                       rhs=skd[:, h, :], start=True, stop=True)
                    mm.then_inc(sc_full, 1)
            pe.wait_ge(sc_done, 8)
            for t in range(TT):
                for n in range(2):
                    mm = pe.matmul(PB[2 + 2 * t + n][:, :], lhsT=zeros[:, :], rhs=XN[:, t, 0:512], start=True,
                                   stop=False, skip_group_check=True)
                if t == 0:
                    mm.then_inc(uv_used, UVB)
                with pe.Fori(0, NSLOT // UVB) as i:
                    for j in range(UVB):
                        pe.wait_ge(diag_done, i * UVB + (t * NSLOT + j + 1))
                        for n in range(2):
                            mm = pe.matmul(PB[2 + 2 * t + n][:, :], lhsT=diag[:, j, :],
                                           rhs=uv[j][:, 1, n * 512:(n + 1) * 512], start=False, stop=False,
                                           skip_group_check=True)
                        mm.then_inc(uv_used, 1)

            def ffn(f):
                n, u0, a0 = N_FFN[f], ffn_base[f], FU * f

                def gate_up(j, i=0):
                    pe.wait_ge(gu_lo_done, i * NS + (a0 + j + 1))
                    pe.wait_ge(a_done, i * NS + (a0 + j + 1))
                    for b in range(2):
                        for k in range(DC):
                            o = (b * DC + k) * P
                            for m, (w, h) in enumerate(products):
                                mm = pe.matmul(PB[j % 2][:, b * T:(b + 1) * T], lhsT=w[:, j % 2, o:o + P],
                                               rhs=h[:, k, :], start=(k == 0 and m == 0),
                                               stop=(k == DC - 1 and m == 2))
                    mm.then_inc(gu_done, 1)

                def down(j, i=0, stop=False):
                    pe.wait_ge(a_done, i * NS + (a0 + j + 3))
                    pe.wait_ge(dn_lo_done, i * NS + (a0 + j + 1))
                    for t in range(TT):
                        for h in range(2):
                            for m, (x, w) in enumerate(((a_hi, dn_hi), (a_hi, dn_lo), (a_lo, dn_hi))):
                                mm = pe.matmul(PB[2 + 2 * t + h][:, :], lhsT=x[:, j % 2, t * P:(t + 1) * P],
                                               rhs=w[:, j % 2, h * 512:(h + 1) * 512],
                                               start=False, stop=(stop and m == 2), skip_group_check=True)
                    mm.then_inc(unit_done, 1)

                transposes(n)
                h_ready(n)
                gate_up(0)
                for t in range(TT):
                    for h in range(2):
                        pe.matmul(PB[2 + 2 * t + h][:, :], lhsT=zeros[:, :], rhs=X[:, t, 0:512],
                                  start=True, stop=False, skip_group_check=True)
                with pe.Fori(0, LOOPS) as i:
                    for j in range(NS):
                        gate_up(j + 1, i)
                        down(j, i)
                for j in range(LOOPS * NS, FU):
                    if j + 1 < FU:
                        gate_up(j + 1)
                    down(j, stop=(j == FU - 1))

            ffn(0)
            transposes(N_S5)
            h_ready(N_S5)
            pe.wait_ge(a_done, FU + 2)
            split_chunks("s5in", 4, lambda c: pe.wait_ge(u_done, c - 1) if c >= 2 else None)
            pe.wait_ge(u_done, 8)
            pe.wait_ge(x_done, 12)
            pe.wait_ge(tab_ready, 2)

            def s5_in(i):
                half, q = i // 8, i % 8
                u = UNIT[("s5b", i // 2)]
                if q % 2 == 0:
                    here(u)
                if i >= 2:
                    pe.wait_ge(v_parts, i - 1)
                for b in range(2):
                    for j in range(4):
                        o = (((q % 2) * 2 + b) * 4 + j) * P
                        mm = pe.matmul(PB[2 + 2 * (i % 2) + b][:, j * P:(j + 1) * P], lhsT=ring[:, u % NS, o:o + P],
                                       rhs=uT[:, q, half * HALF:(half + 1) * HALF], start=True, stop=True)
                    if b == 0 and q % 2 == 1:
                        continue
                if q % 2 == 0:
                    mm.then_inc(bu_full, 1)
                else:
                    mm.then_inc(unit_done, 1)

            def s5_out(i):
                q = i % 8
                pe.wait_ge(o_ready, i + 1)
                if i >= 2:
                    pe.wait_ge(y_done, i - 1)
                for j in range(4):
                    for m, (c, o) in enumerate(((0, 0), (1, 1), (2, 2), (2, 3))):
                        mm = pe.matmul(PB[6 + i % 2][32 * j:32 * j + 32, 0:HALF],
                                       lhsT=CC[:, c, 4 * q + j, :], rhs=s5w[:, 4 + 4 * (i % 2) + o, j, :],
                                       start=(m == 0), stop=(m == 3), skip_group_check=True)
                mm.then_inc(y_full, 1)

            s5_in(0)
            for i in range(16):
                if i + 1 < 16:
                    s5_in(i + 1)
                s5_out(i)
            pe.wait_ge(g_ready, 1)
            chunks("glu", 4, gT, lambda c: pe.wait_ge(sig_done, c - 1) if c >= 2 else None)
            pe.wait_ge(g2_done, 8)
            natural("s5out", yT)
            ffn(1)
            ffn(2)
            transposes(N_MOBA)
            h_ready(N_MOBA)
            for m in range(6):
                if m >= 2:
                    pe.wait_ge(mq_act, m - 1)
                    pe.wait_ge(mq_dve, m - 1)
                for i in range(2):
                    w_part = SPLIT[("qkv", 2 * m + i)]
                    pe.wait_ge(pw_lo_done, w_part + 1)
                    for kk in range(4):
                        k = 4 * i + kk
                        for t in range(TT):
                            for p_, (w, h) in enumerate(products):
                                mm = pe.matmul(PB[2 + 2 * (m % 2) + t][:, :], lhsT=h[:, k, t * P:(t + 1) * P],
                                               rhs=w[:, w_part % 2, kk * 512:(kk + 1) * 512],
                                               start=(k == 0 and p_ == 0), stop=(k == DC - 1 and p_ == 2))
                    mm.then_inc(unit_done, 1)
            pe.wait_ge(qk_ready, 2)
            for i in range(8):
                if i >= 2:
                    pe.wait_ge(mqT_dve if i % 2 else mqT_act, i // 2)
                for j in range(2):
                    for t in range(TT):
                        mm = pe.transpose(PB[6 + i % 2][:, j * T + t * P:j * T + (t + 1) * P],
                                          qkv[:, t, 2 * i + j, :], ident[:, :])
                mm.then_inc(mqT_full, 1)
            pe.wait_ge(mqT_act, 4)
            pe.wait_ge(mqT_dve, 4)
            pe.wait_ge(mq_act, 6)
            pe.wait_ge(mq_dve, 6)
            for t in range(TT):
                S = (t + 1) * P
                if t:
                    pe.wait_ge(L_done, 12)
                for h in range(MH):
                    mm = pe.matmul(PB[2 + h // 2][:, (h % 2) * T:(h % 2) * T + S], lhsT=mqT[:, h, t * P:(t + 1) * P],
                                   rhs=mkT[:, h, 0:S], start=True, stop=True)
                mm.then_inc(lg_full, 1)
                pe.wait_ge(p_ready, 3 + t)
                for s in range(t + 1):
                    if t + s > 0:
                        pe.wait_ge(pt_act, 3 + t + s)
                        pe.wait_ge(pt_dve, 3 + t + s)
                    for r in range(2):
                        for j in range(4):
                            mm = pe.transpose(PB[6 + r][:, j * P:(j + 1) * P], mL[:, 4 * r + j, s * P:(s + 1) * P],
                                              ident[:, :])
                        mm.then_inc(pt_full, 1)
                pe.wait_ge(pt_act, 4 + 2 * t)
                pe.wait_ge(pt_dve, 4 + 2 * t)
                if t:
                    pe.wait_ge(av_done, 3)
                for r in range(2):
                    for j in range(4):
                        for s in range(t + 1):
                            mm = pe.matmul(PB[r][:, j * P:(j + 1) * P], lhsT=qkv[:, s, 16 + 4 * r + j, :],
                                           rhs=mPT[:, s, r, j * P:(j + 1) * P], start=(s == 0), stop=(s == t))
                mm.then_inc(av_full, 1)
            pe.wait_ge(av_done, 4)
            natural("mo", moT)
            ffn(3)

        @block.vector
        def _(dve):
            v = nc.vector
            count = Count()

            def tell(ins, s):
                ins.then_inc(s, 1)
                dve.wait_ge(s, count.up(s))

            def note(ins, s):
                ins.then_inc(s, 1)
                count.up(s)

            def link(ins):
                tell(ins, dve_link)

            def newton(r, root, var, tmp_, s):
                link(v.reciprocal(r, root))
                link(v.tensor_tensor(tmp_, r, r, ALU.mult))
                link(v.scalar_tensor_tensor(out=tmp_, in0=tmp_, scalar=-0.5, in1=var, op0=ALU.mult, op1=ALU.mult))
                tell(v.scalar_tensor_tensor(out=r, in0=tmp_, scalar=1.5, in1=r, op0=ALU.add, op1=ALU.mult), s)

            def norm(n, meanwhile=lambda: None):
                for t in range(TT):
                    ins = v.tensor_tensor_reduce(out=XN[:, t, :], in0=X[:, t, :], in1=X[:, t, :], scale=1.0, scalar=0.0,
                                                 op0=ALU.mult, op1=ALU.add, accum_out=stat[:, t:t + 1])
                link(ins)
                tell(v.tensor_scalar(stat[:, 2:4], stat[:, 0:2], 1.0 / D, EPS, ALU.mult, ALU.add), var_ready)
                meanwhile()
                dve.wait_ge(root_ready, n + 1)
                newton(stat[:, 6:8], stat[:, 4:6], stat[:, 2:4], stat[:, 8:10], rstd_ready)
                tell(v.tensor_scalar(XN[:, 1, :], X[:, 1, :], stat[:, 7:8], None, ALU.mult), xn_dve)

            def evac_h(n, scale, shift):
                for q in (0, 2):
                    dve.wait_ge(tr_full, 4 * n + q + 1)
                    for j in range(2):
                        dc = 2 * q + j
                        src = PB[6][:, j * T:(j + 1) * T]
                        if scale is None:
                            ins = v.tensor_copy(hT[:, dc, :], src)
                        elif shift is None:
                            ins = v.tensor_scalar(hT[:, dc, :], src, scale[:, dc:dc + 1], None, ALU.mult)
                        else:
                            ins = v.tensor_scalar(hT[:, dc, :], src, scale[:, dc:dc + 1], shift[:, dc:dc + 1],
                                                  ALU.mult, ALU.add)
                        tell(ins, hT_dve)

            def gain(n):
                return col("gain")[:, (n - 2) * DC:(n - 1) * DC]

            def split_h(n):
                for q in range(4):
                    if q % 2:
                        dve.wait_ge(hT_act, 4 * n + 2 * (q // 2) + 2)
                    else:
                        dve.wait_ge(tr_full, 4 * n + q + 1)
                        for dc in (2 * q, 2 * q + 1):
                            note(v.tensor_scalar(h_hi[:, dc, :], PB[6][:, (dc % 2) * T:(dc % 2 + 1) * T],
                                                 gain(n)[:, dc:dc + 1], None, ALU.mult), hs_dve)
                        dve.wait_ge(hs_dve, count.n[hs_dve.name])
                    for dc in (2 * q, 2 * q + 1):
                        note(v.scalar_tensor_tensor(out=h_lo[:, dc, :], in0=PB[6 + q % 2][:, (dc % 2) * T:(dc % 2 + 1) * T],
                                                    scalar=gain(n)[:, dc:dc + 1], in1=h_hi[:, dc, :].bitcast(F32),
                                                    op0=ALU.mult, op1=ALU.subtract), hs_dve)

            def trail(name, i):
                p = SPLIT[(name, i)]
                dve.wait_ge(pw_hi_done, p + 1)
                v.tensor_tensor(gu_lo[:, p % 2, :], ring[:, UNIT[(name, i)] % NS, 0:2 * D],
                                gu_hi[:, p % 2, :].bitcast(F32), ALU.subtract).then_inc(pw_lo_done, 1)

            def ada_units(i0, i1):
                for i in range(i0, i1):
                    u = UNIT[("ada", i)]
                    dve.wait_ge(w_here[u % NS], 16 * (u // NS + 1))
                    acc = accA[:, (i // 2) * ADW:(i // 2 + 1) * ADW]
                    for kk in range(4):
                        k = 4 * (i % 2) + kk
                        w, ck = ring[:, u % NS, kk * ADW:(kk + 1) * ADW], col("c")[:, k:k + 1]
                        if k == 0:
                            ins = v.tensor_scalar(acc, w, ck, None, ALU.mult)
                        else:
                            ins = v.scalar_tensor_tensor(out=acc, in0=w, scalar=ck, in1=acc, op0=ALU.mult, op1=ALU.add)
                        tell(ins, unit_done if kk == 3 else dve_link)

            link(v.memset(ones[:, :], 1.0))
            link(v.memset(zeros[:, :], 0.0))
            for j in range(2):
                tell(v.memset(act_a[:, :], 0.0), a_done)

            dve.wait_ge(small_here, 16 * 4)
            dve.wait_ge(ident_ready, 2)
            ada_units(0, 4)
            dt_, mag, f1, f16, f128 = (s5p[:, i, :] for i in range(5))
            t0, t1, t2 = s5p[:, 5, :], s5p[:, 6, :], s5p[:, 7, :]
            cf_re, cf_im, c128, s128 = s5p[:, 8, :], s5p[:, 9, :], s5p[:, 10, :], s5p[:, 11, :]

            def turn(x, scratch):
                link(v.tensor_scalar(scratch, x, MAGIC, MAGIC, ALU.add, ALU.subtract))
                link(v.tensor_tensor(x, x, scratch, ALU.subtract))

            dve.wait_ge(ang_ready, 1)
            link(v.tensor_tensor(t0, col("a_re"), dt_, ALU.mult))
            link(v.tensor_tensor(f1, col("a_im"), dt_, ALU.mult))
            link(v.tensor_scalar(f1, f1, 1.0 / (2.0 * np.pi), None, ALU.mult))
            turn(f1, t1)
            link(v.tensor_scalar(f16, f1, 16.0, None, ALU.mult))
            turn(f16, t1)
            link(v.tensor_scalar(f128, f1, float(HALF), None, ALU.mult))
            turn(f128, t1)
            sc4 = arena[:, 4096:4096 + NPAIR * 16].rearrange("p (a b) -> p a b", b=16)
            for b, f in ((0, f1), (2, f16)):
                m = 16 if b == 0 else 8
                link(v.tensor_tensor(base[b + 1], f.unsqueeze(2).broadcast_to([P, NPAIR, m]),
                                     iota16[:, 0:m].unsqueeze(1).broadcast_to([P, NPAIR, m]), ALU.mult))
                link(v.tensor_scalar(base[b], base[b + 1], 0.25, None, ALU.add))
                turn(base[b], sc4[:, :, 0:m])
                turn(base[b + 1], sc4[:, :, 0:m])
            link(v.tensor_copy(s128, f128))
            link(v.tensor_scalar(c128, f128, 0.25, None, ALU.add))
            turn(c128, t1)
            tell(v.tensor_copy(t2, t0), s5p_ready)
            ada_units(4, 8)
            dve.wait_ge(trig_ready, 1)
            lre, lim = s5p[:, 12, :], s5p[:, 13, :]
            link(v.tensor_tensor(lre, mag, base[0][:, :, 1], ALU.mult))
            link(v.tensor_tensor(lim, mag, base[1][:, :, 1], ALU.mult))
            link(v.tensor_scalar(lre, lre, 1.0, None, ALU.subtract))
            link(v.tensor_tensor(t0, col("a_re"), col("a_re"), ALU.mult))
            link(v.tensor_tensor(t1, col("a_im"), col("a_im"), ALU.mult))
            link(v.tensor_tensor(t0, t0, t1, ALU.add))
            link(v.reciprocal(t2, t0))
            link(v.tensor_tensor(t0, lre, col("a_re"), ALU.mult))
            link(v.tensor_tensor(t1, lim, col("a_im"), ALU.mult))
            link(v.tensor_tensor(t0, t0, t1, ALU.add))
            link(v.tensor_tensor(cf_re, t0, t2, ALU.mult))
            link(v.tensor_tensor(t0, lim, col("a_re"), ALU.mult))
            link(v.tensor_tensor(t1, lre, col("a_im"), ALU.mult))
            link(v.tensor_tensor(t0, t0, t1, ALU.subtract))
            tell(v.tensor_tensor(cf_im, t0, t2, ALU.mult), s5p_ready)
            dve.wait_ge(ident_ready, 3)
            for g in range(4):
                link(v.tensor_scalar(rcnt[:, g, :], iotai[:, :], 2.0 ** (g + 1), None, ALU.min))
            tell(v.reciprocal(rcnt[:, :, :], rcnt[:, :, :]), rcnt_ready)

            dve.wait_ge(x_here, 16)
            norm(0)
            ada_units(8, 16)
            dve.wait_ge(ada_full, 1)
            tell(v.tensor_tensor(ada[:, :, :].rearrange("p a b -> p (a b)"), PB[6][:, 0:6 * DC], col("b_ada"), ALU.add),
                 ada_ready)
            tell(v.scalar_tensor_tensor(out=A1[:, :], in0=ada[:, 1, :], scalar=1.0, in1=col("g1"), op0=ALU.add,
                                        op1=ALU.mult), ada_ready)
            tell(v.scalar_tensor_tensor(out=A2[:, :], in0=ada[:, 4, :], scalar=1.0, in1=col("g2"), op0=ALU.add,
                                        op1=ALU.mult), ada_ready)
            evac_h(0, A1[:, :], ada[:, 0, :])

            dve.wait_ge(unit_done, UNIT[("nat", 1)] + 1)
            for t in range(TT):
                src = PB[4 + t]
                for c in range(4):
                    link(v.tensor_copy(zq[:, t, 8 + c, :], src[:, (c // 2) * HD:(c // 2 + 1) * HD]))
                link(v.tensor_copy(vn[:, t, :], src[:, 2 * HD:3 * HD]))
                tell(v.tensor_scalar(iw[:, t, :], src[:, 3 * HD:3 * HD + IH], IH ** -0.5, None, ALU.mult), nat_out)
            dve.wait_ge(natq_out, TT)

            def head_norm(z, z2, hd, nh, n):
                link(v.tensor_tensor(z2, z, z, ALU.mult))
                link(v.tensor_reduce(hstat[:, 0, 0:nh], z2, AX_X, ALU.add))
                tell(v.tensor_scalar(hstat[:, 0, 0:nh], hstat[:, 0, 0:nh], 1.0 / hd, EPS, ALU.mult, ALU.add), hvar_ready)
                dve.wait_ge(hroot_ready, n)
                newton(hstat[:, 2, 0:nh], hstat[:, 1, 0:nh], hstat[:, 0, 0:nh], hstat[:, 3, 0:nh], dve_link)
                link(v.tensor_tensor(z, z, hstat[:, 2, 0:nh].unsqueeze(2).broadcast_to([P, nh, hd]), ALU.mult))

            zf = zq.rearrange("p t h d -> p (t h) d")
            head_norm(zf, sq.rearrange("p t h d -> p (t h) d"), HD, 24, 1)
            for h0, h1, b in ((0, 8, 0), (8, 10, 1), (10, 12, 2)):
                zt = zq[:, :, h0:h1, :]
                gb = rows[:, b * HD:(b + 1) * HD].unsqueeze(1).unsqueeze(1).broadcast_to([P, TT, h1 - h0, HD])
                ins = v.tensor_tensor(zt, zt, gb, ALU.mult)
                if b < 2:
                    link(ins)
                else:
                    tell(ins, qk_ready)

            for t in range(TT):
                S = (t + 1) * P
                dve.wait_ge(rel_done, 2 * t + 2)
                sc0, sc1 = score[:, 0, 0:S], score[:, 1, 0:S]
                link(v.tensor_scalar(sc0, rel[:, 0, 0:S], iw[:, t, 0:1], None, ALU.mult))
                for plane, h in ((2, 1), (1, 2), (3, 3)):
                    link(v.scalar_tensor_tensor(out=sc0, in0=rel[:, plane, 0:S], scalar=iw[:, t, h:h + 1], in1=sc0,
                                                op0=ALU.mult, op1=ALU.add))
                link(v.memset(score[0:64, 0, S - 64:S], NEG))
                for r in range(TOPK // 8):
                    link(v.max(top8[:, :], sc0))
                    link(v.match_replace(out=sc0, in_to_replace=top8[:, :], in_values=sc0, imm_value=GONE))
                tell(v.tensor_scalar(maskb[:, t, 0:S], sc0, -2e38, NEG, ALU.is_gt, ALU.mult), mask_ready)

            def softmax_head(base, t, Lt, S, groups, scale, masks):
                dve.wait_ge(lg_full, base + t + 1)
                for g, dst in enumerate(groups):
                    masks(g, dst)
                link(v.tensor_reduce(rmax[:, 0, :], Lt[:, :, 0:S], AX_X, ALU.max))
                tell(v.tensor_scalar(rmax[:, 1, :], rmax[:, 0, :], -scale, None, ALU.mult), nm_ready)
                dve.wait_ge(exp_done, base + t + 1)
                link(v.reciprocal(rmax[:, 3, :], rmax[:, 2, :]))
                tell(v.tensor_tensor(Lt[:, :, 0:S], Lt[:, :, 0:S], rmax[:, 3, :].unsqueeze(2).broadcast_to([P, NH, S]),
                                     ALU.mult), p_ready)

            Lv = L.rearrange("p (jj hf r) s -> p jj hf r s", jj=2, hf=2)
            for t in range(TT):
                S = (t + 1) * P

                def masks(g, dst, S=S, t=t):
                    r, jj = g % 2, g // 2
                    src = PB[2 + g][:, :].rearrange("p (a s) -> p a s", a=2)[:, :, 0:S]
                    tell(v.tensor_tensor(Lv[:, jj, :, r, 0:S], src,
                                         maskb[:, t, 0:S].unsqueeze(1).broadcast_to([P, 2, S]), ALU.add), L_done)

                softmax_head(0, t, L, S, range(4), HD ** -0.5, masks)
                for s in range(t + 1):
                    dve.wait_ge(pt_full, 2 * (t + s) + 2)
                    tell(v.tensor_copy(PT[:, s, 1, :], PB[7][:, :]), pt_dve)
                dve.wait_ge(av_full, t + 1)
                tell(v.tensor_copy(yat[:, :, t * P:(t + 1) * P], PB[t][:, :].rearrange("p (j q) -> p j q", j=4)),
                     av_done)

            for dc in range(DC):
                i, c = dc // 2, dc % 2
                if c == 0:
                    dve.wait_ge(half_done, HALVES[("up", i)] + 1)
                else:
                    dve.wait_ge(unit_done, UNIT[("up", i)] + 1)
                link(v.tensor_tensor(tmp[:, 0, 0:T], PB[c][:, 0:T], sg[:, dc, :], ALU.mult))
                link(v.tensor_tensor(tmp[:, 1, 0:T], PB[c][:, T:2 * T], sg[:, DC + dc, :], ALU.mult))
                tell(v.tensor_tensor(mixT[:, dc, :], tmp[:, 0, 0:T], tmp[:, 1, 0:T], ALU.add), mixT_done)

            def residual(row):
                for t in range(TT):
                    for n in range(2):
                        xs = X[:, t, n * 512:(n + 1) * 512]
                        link(v.tensor_tensor(tmp[:, n, :], PB[2 + 2 * t + n][:, :], brow[:, row, n * 512:(n + 1) * 512],
                                             ALU.mult))
                        tell(v.tensor_tensor(xs, xs, tmp[:, n, :], ALU.add), x_done)

            def residual_plain(scale):
                for t in range(TT):
                    for n in range(2):
                        xs = X[:, t, n * 512:(n + 1) * 512]
                        ins = v.scalar_tensor_tensor(out=xs, in0=PB[2 + 2 * t + n][:, :], scalar=scale, in1=xs,
                                                     op0=ALU.mult, op1=ALU.add)
                        if t == TT - 1 and n == 1:
                            tell(ins, x_done)
                        else:
                            note(ins, x_done)

            dve.wait_ge(unit_done, UNIT[("wo", 3)] + 1)
            residual(0)
            norm(1)
            dve.wait_ge(xn_act, 2)
            for t in range(TT):
                link(v.tensor_tensor(XN[:, t, :], XN[:, t, :], brow[:, 1, :], ALU.mult))
                tell(v.tensor_tensor(XN[:, t, :], XN[:, t, :], brow[:, 2, :], ALU.add), h2_ready)
            evac_h(1, None, None)

            def top16(vals, idx, src):
                link(v.max(vals[:, 0:8], src))
                link(v.max_index(idx[:, 0:8], vals[:, 0:8], src))
                wk = work[:, 0:src.shape[1]]
                link(v.match_replace(out=wk, in_to_replace=vals[:, 0:8], in_values=src, imm_value=GONE))
                link(v.max(vals[:, 8:16], wk))
                link(v.max_index(idx[:, 8:16], vals[:, 8:16], wk))

            def top_keys(t, heads):
                for h in heads:
                    if h % 4 == 0:
                        dve.wait_ge(sc_done, 4 * t + h // 4 + 1)
                    top16(tv[:, h, :], ti[:, h, :], sco[:, t, h, :])

            def pair_sums():
                link(v.tensor_copy(tif[:, :, :], ti[:, :, :]))
                tvv = tv[:, :, :].rearrange("p (h two) k -> p h two k", two=2)
                cv = cand.rearrange("p h (x y) -> p h x y", y=PK)
                link(v.tensor_tensor(cv, tvv[:, :, 0, :].unsqueeze(3).broadcast_to([P, PH, PK, PK]),
                                     tvv[:, :, 1, :].unsqueeze(2).broadcast_to([P, PH, PK, PK]), ALU.add))

            def top_sums(heads):
                for h in heads:
                    top16(bv[:, h, :], bp[:, h * PK:(h + 1) * PK], cand[:, h, :])

            def gate_inputs(t):
                tell(v.tensor_tensor(gate[:, t, :, :], bv[:, :, :], bv[:, :, 0:1].broadcast_to([P, PH, PK]),
                                     ALU.subtract), gx_ready)
                link(v.tensor_scalar(bq[:, 0, :], bp[:, :], 4, None, ALU.logical_shift_right))
                link(v.tensor_scalar(bq[:, 1, :], bp[:, :], PK - 1, None, ALU.bitwise_and))
                link(v.tensor_copy(bqf[:, :, :], bq[:, :, :]))

            def key_numbers(b):
                tifv = tif[:, :, :].rearrange("p (h two) k -> p h two k", two=2)
                link(v.tensor_tensor(oneh, bqf[:, b, :].unsqueeze(2).broadcast_to([P, NSLOT, PK]),
                                     iota16[:, :].unsqueeze(1).broadcast_to([P, NSLOT, PK]), ALU.is_equal))
                o4 = oneh.rearrange("p (h k) x -> p h k x", h=PH)
                link(v.tensor_tensor(o4, o4, tifv[:, :, b, :].unsqueeze(2).broadcast_to([P, PH, PK, PK]), ALU.mult))
                link(v.tensor_reduce(ei[:, b, :], oneh, AX_X, ALU.add))

            def experts(t):
                link(v.scalar_tensor_tensor(out=ei[:, 0, :], in0=ei[:, 0, :], scalar=float(NKEYS), in1=ei[:, 1, :],
                                            op0=ALU.mult, op1=ALU.add))
                tell(v.tensor_copy(eidx[:, t, :], ei[:, 0, :]), route_ready)
                dve.wait_ge(ge_done, t + 1)
                link(v.tensor_reduce(gst[:, 0, :], gate[:, t, :, :], AX_X, ALU.add))
                link(v.reciprocal(gst[:, 1, :], gst[:, 0, :]))
                link(v.tensor_tensor(gate[:, t, :, :], gate[:, t, :, :],
                                     gst[:, 1, :].unsqueeze(2).broadcast_to([P, PH, PK]), ALU.mult))

            def gathered(t, r, i=0):
                gt = gate[:, t, :, :].rearrange("p h k -> p (h k)")
                for g in range(2):
                    for j in range(4 * g, 4 * g + 4):
                        dve.wait_ge(uv_here[j], i * 16 + (t * (NSLOT // UVB) + r + 1) * 16)
                        v.tensor_tensor_reduce(out=uv[j][:, 0, :], in0=uv[j][:, 0, :], in1=XN[:, t, :], scale=1.0,
                                               scalar=0.0, op0=ALU.mult, op1=ALU.add,
                                               accum_out=dots[:, j:j + 1]).then_inc(dot_done, 1)
                    dve.wait_ge(gelu_done, i * 2 + (2 * (t * (NSLOT // UVB) + r) + g + 1))
                    for j in range(4 * g, 4 * g + 4):
                        slot = r * UVB + j
                        v.tensor_scalar(diag[:, j, :], ident[:, :], gl[:, j:j + 1],
                                        gt[:, slot:slot + 1] if isinstance(i, int) else gt[:, bass.ds(i * UVB + slot, 1)],
                                        ALU.mult, ALU.mult).then_inc(diag_done, 1)

            top_keys(0, range(16))
            pair_sums()
            top_sums(range(PH))
            gate_inputs(0)
            key_numbers(0)
            key_numbers(1)
            experts(0)
            for r in range(ROUTE_ROUNDS):
                gathered(0, r)
                if r < 4:
                    top_keys(1, range(4 * r, 4 * r + 4))
                elif r == 4:
                    pair_sums()
                    top_sums(range(0, 4))
                elif r == EXP_ROUND - 1:
                    top_sums(range(4, PH))
                    gate_inputs(1)
                elif r == 6:
                    key_numbers(0)
                else:
                    key_numbers(1)
                    experts(1)
            with dve.Fori(0, NSLOT // UVB - ROUTE_ROUNDS) as i:
                gathered(0, ROUTE_ROUNDS, i)
            with dve.Fori(0, NSLOT // UVB) as i:
                gathered(1, 0, i)
            dve.wait_ge(diag_done, TT * NSLOT)
            count.n[diag_done.name] = TT * NSLOT
            dve.wait_ge(uv_used, TT * NSLOT + UVB)
            link(v.tensor_copy(stat[:, 10:11], stat[:, 9:10]))
            residual(3)

            def ffn(f):
                n, u0, a0 = N_FFN[f], ffn_base[f], FU * f
                def split_gate_up(j, i=0):
                    dve.wait_ge(gu_hi_done, i * NS + (a0 + j + 1))
                    v.tensor_tensor(gu_lo[:, j % 2, :], ring[:, (u0 + j) % NS, 0:2 * D], gu_hi[:, j % 2, :].bitcast(F32),
                                    ALU.subtract).then_inc(gu_lo_done, 1)

                def split_down(j, i=0):
                    dve.wait_ge(dn_hi_done, i * NS + (a0 + j + 1))
                    v.tensor_tensor(dn_lo[:, j % 2, :], ring[:, (u0 + j) % NS, 2 * D:3 * D],
                                    dn_hi[:, j % 2, :].bitcast(F32), ALU.subtract).then_inc(dn_lo_done, 1)

                def activation(j, i=0):
                    dve.wait_ge(silu_done, i * NS + (a0 + j + 1))
                    dve.wait_ge(a_done, i * NS + (a0 + j + 2))
                    v.tensor_tensor(act_a[:, :], PB[j % 2][:, T:2 * T], act_gs[:, j % 2, :],
                                    ALU.mult).then_inc(prod_done, 1)
                    dve.wait_ge(prod_done, i * NS + (a0 + j + 1))
                    dve.wait_ge(unit_done, i * NS + (u0 + j - 1))
                    v.tensor_copy(a_hi[:, j % 2, :], act_a[:, :]).then_inc(a_hi_done, 1)
                    dve.wait_ge(a_hi_done, i * NS + (a0 + j + 1))
                    v.tensor_tensor(a_lo[:, j % 2, :], act_a[:, :], a_hi[:, j % 2, :].bitcast(F32),
                                    ALU.subtract).then_inc(a_done, 1)

                norm(n, lambda: split_gate_up(0))
                split_h(n)
                with dve.Fori(0, LOOPS) as i:
                    for j in range(NS):
                        split_gate_up(j + 1, i)
                        activation(j, i)
                        split_down(j, i)
                for j in range(LOOPS * NS, FU):
                    if j + 1 < FU:
                        split_gate_up(j + 1)
                    activation(j)
                    split_down(j)
                dve.wait_ge(unit_done, u0 + FU)
                dve.wait_ge(a_done, a0 + FU + 2)
                count.n[a_done.name] = a0 + FU + 2
                residual_plain(0.5)

            ffn(0)
            norm(N_S5, lambda: trail("s5in", 0))
            split_h(N_S5)
            for i in range(1, 4):
                trail("s5in", i)
            dve.wait_ge(tab_ready, 2)
            for i in range(16):
                half, q = i // 8, i % 8
                if q % 2 == 0:
                    dve.wait_ge(bu_full, half * 4 + q // 2 + 1)
                else:
                    dve.wait_ge(unit_done, UNIT[("s5b", i // 2)] + 1)
                re = PB[2 + 2 * (i % 2)][:, :].rearrange("p (j s) -> p j s", j=4)
                im = PB[3 + 2 * (i % 2)][:, :].rearrange("p (j s) -> p j s", j=4)
                ec, es = Ec[:, 4 * q:4 * q + 4, :], Es[:, 4 * q:4 * q + 4, :]
                vr, vi, m0, m1 = (s5w[:, k, :, :] for k in (0, 1, 12, 13))
                v.tensor_tensor(vr, re, ec, ALU.mult)
                v.tensor_tensor(m0, im, es, ALU.mult)
                v.tensor_tensor(vi, im, ec, ALU.mult)
                tell(v.tensor_tensor(m1, re, es, ALU.mult), v_parts)
                v.tensor_tensor(vr, vr, m0, ALU.add)
                link(v.tensor_tensor(vi, vi, m1, ALU.subtract))
                if i >= 2:
                    dve.wait_ge(o_ready, i - 1)
                for b, vv in ((0, vr), (1, vi)):
                    ww = s5w[:, W_AT[i % 2] + b, :, :]
                    for j in range(4):
                        pair = 4 * q + j
                        init = 0.0 if half == 0 else s5p[:, 14 + b, pair:pair + 1]
                        ins = v.tensor_tensor_scan(ww[:, j, :], mag[:, pair:pair + 1].broadcast_to([P, HALF]), vv[:, j, :],
                                                   init, ALU.mult, ALU.add)
                        if b == 1 and j == 3:
                            tell(ins, w_ready)
                if half == 0:
                    wr, wi = (s5w[:, W_AT[i % 2] + b, :, HALF - 1] for b in range(2))
                    ps = slice(4 * q, 4 * q + 4)
                    v.tensor_tensor(t0[:, ps], wr, c128[:, ps], ALU.mult)
                    link(v.tensor_tensor(t1[:, ps], wi, s128[:, ps], ALU.mult))
                    link(v.tensor_tensor(s5p[:, 14, ps], t0[:, ps], t1[:, ps], ALU.subtract))
                    v.tensor_tensor(t0[:, ps], wr, s128[:, ps], ALU.mult)
                    link(v.tensor_tensor(t1[:, ps], wi, c128[:, ps], ALU.mult))
                    link(v.tensor_tensor(s5p[:, 15, ps], t0[:, ps], t1[:, ps], ALU.add))
                for k in range(max(i - 2, 0), 16 if i == 15 else i - 1):
                    hk, qk = k // 8, k % 8
                    dve.wait_ge(y_full, k + 1)
                    ts = slice(hk * HALF, (hk + 1) * HALF)
                    tell(v.scalar_tensor_tensor(out=yT[:, qk, ts], in0=uT[:, qk, ts], scalar=col("d_skip")[:, qk:qk + 1],
                                                in1=PB[6 + k % 2][:, 0:HALF], op0=ALU.mult, op1=ALU.add), y_done)
            for c in range(DC):
                dve.wait_ge(sig_done, c + 1)
                tell(v.tensor_tensor(yT[:, c, :], yT[:, c, :], gT[:, c, :], ALU.mult), g2_done)
            dve.wait_ge(unit_done, UNIT[("s5out", 3)] + 1)
            residual_plain(1.0)
            ffn(1)
            ffn(2)

            norm(N_MOBA, lambda: trail("qkv", 0))
            split_h(N_MOBA)
            trail("qkv", 1)
            for m in range(6):
                if m < 5:
                    trail("qkv", 2 * m + 2)
                dve.wait_ge(unit_done, UNIT[("qkv", 2 * m + 1)] + 1)
                tell(v.tensor_copy(qkv[:, 1, 4 * m:4 * m + 4, :],
                                   PB[3 + 2 * (m % 2)][:, :].rearrange("p (h d) -> p h d", h=4)), mq_dve)
                if m < 5:
                    trail("qkv", 2 * m + 3)
                if m == 3:
                    dve.wait_ge(mq_act, 4)
                    for t in range(TT):
                        z = qkv[:, t, 0:16, :]
                        link(v.tensor_tensor(msq[:, t, :, :], z, z, ALU.mult))
                        link(v.tensor_reduce(hstat[:, 0, 16 * t:16 * t + 16], msq[:, t, :, :], AX_X, ALU.add))
                    tell(v.tensor_scalar(hstat[:, 0, :], hstat[:, 0, :], 1.0 / MD, EPS, ALU.mult, ALU.add), hvar_ready)
            dve.wait_ge(hroot_ready, 2)
            newton(hstat[:, 2, :], hstat[:, 1, :], hstat[:, 0, :], hstat[:, 3, :], dve_link)
            for t in range(TT):
                z = qkv[:, t, 0:16, :]
                link(v.tensor_tensor(z, z, hstat[:, 2, 16 * t:16 * t + 16].unsqueeze(2).broadcast_to([P, 16, MD]),
                                     ALU.mult))
                zz = z.rearrange("p (a h) d -> p a h d", a=2)
                mg = rows[:, 3 * HD:3 * HD + 2 * MD].rearrange("p (a d) -> p a d", a=2)
                link(v.tensor_tensor(zz, zz, mg.unsqueeze(2).broadcast_to([P, 2, MH, MD]), ALU.mult))
                x1, x2 = z[:, :, 0:ROT], z[:, :, ROT:2 * ROT]
                cs = rope[:, t, 0, :].unsqueeze(1).broadcast_to([P, 16, ROT])
                sn = rope[:, t, 1, :].unsqueeze(1).broadcast_to([P, 16, ROT])
                r = [mrt[:, k, 0:16, :] for k in range(4)]
                link(v.tensor_tensor(r[0], x1, cs, ALU.mult))
                link(v.tensor_tensor(r[1], x2, sn, ALU.mult))
                link(v.tensor_tensor(r[2], x2, cs, ALU.mult))
                link(v.tensor_tensor(r[3], x1, sn, ALU.mult))
                link(v.tensor_tensor(x1, r[0], r[1], ALU.subtract))
                if t == 0:
                    link(v.tensor_tensor(x2, r[2], r[3], ALU.add))
                else:
                    tell(v.tensor_tensor(x2, r[2], r[3], ALU.add), qk_ready)
            for i in (1, 3, 5, 7):
                dve.wait_ge(mqT_full, i + 1)
                dst = (mqT if i < 4 else mkT)[:, 2 * (i % 4):2 * (i % 4) + 2, :]
                tell(v.tensor_copy(dst, PB[7][:, :].rearrange("p (h q) -> p h q", h=2)), mqT_dve)
            dve.wait_ge(causal_ready, 1)
            for t in range(TT):
                S = (t + 1) * P

                def mmask(g, dst, S=S, t=t):
                    src = PB[2 + g][:, :].rearrange("p (a s) -> p a s", a=2)
                    if t:
                        link(v.tensor_copy(mL[:, 2 * g:2 * g + 2, 0:P], src[:, :, 0:P]))
                    tell(v.tensor_tensor(mL[:, 2 * g:2 * g + 2, S - P:S], src[:, :, S - P:S],
                                         causal.unsqueeze(1).broadcast_to([P, 2, P]), ALU.add), L_done)

                softmax_head(2, t, mL, S, range(4), MD ** -0.5, mmask)
                for s in range(t + 1):
                    dve.wait_ge(pt_full, 6 + 2 * (t + s) + 2)
                    tell(v.tensor_copy(mPT[:, s, 1, :], PB[7][:, :]), pt_dve)
                dve.wait_ge(av_full, 3 + t)
                link(v.tensor_copy(moT[:, 0:4, t * P:(t + 1) * P], PB[0][:, :].rearrange("p (j q) -> p j q", j=4)))
                tell(v.tensor_copy(moT[:, 4:8, t * P:(t + 1) * P], PB[1][:, :].rearrange("p (j q) -> p j q", j=4)),
                     av_done)
            dve.wait_ge(unit_done, UNIT[("mo", 3)] + 1)
            residual_plain(1.0)
            ffn(3)

        @block.scalar
        def _(act):
            s = nc.scalar
            count = Count()

            def tell(ins, sm):
                ins.then_inc(sm, 1)
                act.wait_ge(sm, count.up(sm))

            act.dma_start(cols[:, :], a["cols"]).then_inc(small_here, 16)
            act.dma_start(X[:, :, :], a["x"].rearrange("(t p) d -> p t d", p=P)).then_inc(x_here, 16)
            act.dma_start(rows[:, :], a["rows"].partition_broadcast(P)).then_inc(small_here, 16)
            act.dma_start(rope[:, :, :, :], a["rope"]).then_inc(small_here, 16)
            act.dma_start(wgrp[:, :, :], a["w_grp"]).then_inc(small_here, 16)

            def lead(name, i, after):
                u, p = UNIT[(name, i)], SPLIT[(name, i)]
                act.wait_ge(w_here[u % NS], 16 * (u // NS + 1))
                act.wait_ge(unit_done, after)
                s.copy(gu_hi[:, p % 2, :], ring[:, u % NS, 0:2 * D]).then_inc(pw_hi_done, 1)

            def split_h(n):
                for q in (1, 3):
                    act.wait_ge(tr_full, 4 * n + q + 1)
                    for j in range(2):
                        dc = 2 * q + j
                        tell(s.activation(h_hi[:, dc, :], PB[7][:, j * T:(j + 1) * T], ACT.Copy,
                                          scale=gain(n)[:, dc:dc + 1]), hT_act)

            def norm(n):
                act.wait_ge(var_ready, n + 1)
                tell(s.activation(stat[:, 4:6], stat[:, 2:4], ACT.Sqrt), root_ready)
                act.wait_ge(rstd_ready, n + 1)
                tell(s.activation(XN[:, 0, :], X[:, 0, :], ACT.Copy, scale=stat[:, 6:7]), xn_act)

            def evac_h(n, scale, shift):
                for q in (1, 3):
                    act.wait_ge(tr_full, 4 * n + q + 1)
                    for j in range(2):
                        dc = 2 * q + j
                        src = PB[7][:, j * T:(j + 1) * T]
                        if scale is None:
                            ins = s.copy(hT[:, dc, :], src)
                        elif shift is None:
                            ins = s.activation(hT[:, dc, :], src, ACT.Copy, scale=scale[:, dc:dc + 1])
                        else:
                            ins = s.activation(hT[:, dc, :], src, ACT.Identity, bias=shift[:, dc:dc + 1],
                                               scale=scale[:, dc:dc + 1])
                        tell(ins, hT_act)

            def gain(n):
                return col("gain")[:, (n - 2) * DC:(n - 1) * DC]

            act.wait_ge(small_here, 16 * 4)
            tell(s.activation(s5p[:, 0, :], col("log_dt"), ACT.Exp), ang_ready)
            act.wait_ge(s5p_ready, 1)
            tell(s.activation(s5p[:, 1, :], s5p[:, 7, :], ACT.Exp), act_link)
            for b in range(4):
                m = 16 if b < 2 else 8
                tell(s.activation(base[b], base[b], ACT.Sin, scale=TWO_PI), act_link)
            tell(s.activation(s5p[:, 10:12, :], s5p[:, 10:12, :], ACT.Sin, scale=TWO_PI), trig_ready)
            norm(0)
            for i in range(8):
                act.wait_ge(brow_full, i + 1)
                tell(s.copy(brow[:, i // 2, (i % 2) * 512:(i % 2 + 1) * 512], PB[2 + i % 4][:, :]), brow_done)
            act.wait_ge(ada_ready, 3)
            evac_h(0, A1[:, :], ada[:, 0, :])
            act.wait_ge(unit_done, UNIT[("nat", 1)] + 1)
            for t in range(TT):
                tell(s.copy(zq[:, t, 0:NH, :], PB[2 + t][:, :].rearrange("p (h d) -> p h d", h=NH)), natq_out)
            act.wait_ge(hvar_ready, 1)
            tell(s.activation(hstat[:, 1, 0:24], hstat[:, 0, 0:24], ACT.Sqrt), hroot_ready)
            act.wait_ge(ident_ready, 4)

            def wait_chunk(name, i, c):
                if c == 0:
                    act.wait_ge(half_done, HALVES[(name, i)] + 1)
                else:
                    act.wait_ge(unit_done, UNIT[(name, i)] + 1)

            for c in range(6):
                wait_chunk("tz", c // 2, c % 2)
                dst = iqT[:, c, :] if c < 2 else pT[:, c - 2, 16:16 + T]
                tell(s.copy(dst, PB[c % 2][:, 0:T]), tz_done)
            for c in range(8):
                wait_chunk("zg", c // 2, c % 2)
                tell(s.activation(sg[:, c, :], PB[c % 2][:, 0:T], ACT.Sigmoid), tz_done)
            for p in range(6):
                act.wait_ge(qkT_full, p + 1)
                tell(s.copy(qkT[:, p, :], PB[6 + p % 2][:, 0:T]), qkT_done)

            def relus(t):
                S = (t + 1) * P
                act.wait_ge(idx_full, t + 1)
                if t:
                    act.wait_ge(mask_ready, t)
                for r in range(2):
                    src = PB[2 + 2 * t + r][:, :].rearrange("p (a s) -> p a s", a=2)[:, :, 0:S]
                    tell(s.activation(rel[:, 2 * r:2 * r + 2, 0:S], src, ACT.Relu, scale=HD ** -0.5), rel_done)

            relus(0)
            for c in range(8, 12):
                wait_chunk("zg", c // 2, c % 2)
                tell(s.activation(sg[:, c, :], PB[c % 2][:, 0:T], ACT.Sigmoid), tz_done)
            relus(1)
            for c in range(12, 16):
                wait_chunk("zg", c // 2, c % 2)
                tell(s.activation(sg[:, c, :], PB[c % 2][:, 0:T], ACT.Sigmoid), tz_done)
            for g in range(4):
                act.wait_ge(pg_full, g + 1)
                tell(s.activation(ypT[:, g, :], PB[g % 2][:, 0:T], ACT.Copy, scale=col("s_pool")[:, g:g + 1]), pg_done)

            def softmax(base, t, Lt, S, scale, pt, full):
                act.wait_ge(nm_ready, base + t + 1)
                for h in range(NH):
                    tell(s.activation(Lt[:, h, 0:S], Lt[:, h, 0:S], ACT.Exp, bias=rmax[:, 1, h:h + 1], scale=scale,
                                      accum_out=rmax[:, 2, h:h + 1]), exp_done if h == NH - 1 else act_link)
                for sk in range(t + 1):
                    act.wait_ge(pt_full, full + 2 * (t + sk) + 1)
                    tell(s.copy(pt[:, sk, 0, :], PB[6][:, :]), pt_act)

            for t in range(TT):
                softmax(0, t, L, (t + 1) * P, HD ** -0.5, PT, 0)
            norm(1)
            evac_h(1, None, None)
            act.dma_start(skd[:, :, :], a["skd"]).then_inc(sk_here, 16)
            for c in range(DC):
                wait_chunk("pq", c // 2, c % 2)
                tell(s.copy(pqT[:, c, :], PB[c % 2][:, 0:T]), pq_done)
            for t in range(TT):
                for hp in range(4):
                    act.wait_ge(sc_full, 4 * t + hp + 1)
                    tell(s.copy(sco[:, t, 4 * hp:4 * hp + 4, :], PB[2 + hp][:, :].rearrange("p (h k) -> p h k", h=4)),
                         sc_done)

            def gate_exp(t):
                act.wait_ge(gx_ready, t + 1)
                tell(s.activation(gate[:, t, :, :], gate[:, t, :, :], ACT.Exp), ge_done)

            def gelus(first, rounds):
                with act.Fori(0, rounds) as i:
                    for g in range(2):
                        act.wait_ge(dot_done, i * UVB + (first * UVB + 4 * g + 4))
                        s.activation(gl[:, 4 * g:4 * g + 4], dots[:, 4 * g:4 * g + 4], ACT.Gelu).then_inc(gelu_done, 1)

            gate_exp(0)
            gelus(0, EXP_ROUND)
            gate_exp(1)
            gelus(EXP_ROUND, TT * NSLOT // UVB - EXP_ROUND)

            def ffn(f):
                n, u0, a0 = N_FFN[f], ffn_base[f], FU * f
                def lead_gate_up(j, i=0):
                    u = u0 + j
                    act.wait_ge(w_here[u % NS], i * 16 + 16 * (u // NS + 1))
                    act.wait_ge(a_done, i * NS + (a0 + j + 1))
                    s.copy(gu_hi[:, j % 2, :], ring[:, u % NS, 0:2 * D]).then_inc(gu_hi_done, 1)

                def lead_down(j, i=0):
                    act.wait_ge(unit_done, i * NS + (u0 + j - 1))
                    s.copy(dn_hi[:, j % 2, :], ring[:, (u0 + j) % NS, 2 * D:3 * D]).then_inc(dn_hi_done, 1)

                def silu(j, i=0):
                    act.wait_ge(gu_done, i * NS + (a0 + j + 1))
                    act.wait_ge(a_done, i * NS + (a0 + j + 1))
                    s.activation(act_gs[:, j % 2, :], PB[j % 2][:, 0:T], ACT.Silu).then_inc(silu_done, 1)

                if f == 0:
                    act.wait_ge(uv_used, TT * NSLOT + UVB)
                act.wait_ge(unit_done, u0)
                lead_gate_up(0)
                norm(n)
                split_h(n)
                with act.Fori(0, LOOPS) as i:
                    for j in range(NS):
                        lead_gate_up(j + 1, i)
                        silu(j, i)
                        lead_down(j, i)
                for j in range(LOOPS * NS, FU):
                    if j + 1 < FU:
                        lead_gate_up(j + 1)
                    silu(j)
                    lead_down(j)

            ffn(0)
            lead("s5in", 0, UNIT[("s5in", 0)])
            norm(N_S5)
            split_h(N_S5)
            lead("s5in", 1, UNIT[("s5in", 0)])
            for c in range(DC):
                wait_chunk("s5in", c // 2, c % 2)
                tell(s.copy(uT[:, c, :], PB[c % 2][:, 0:T]), u_done)
                if c % 2 and c // 2 + 2 < 4:
                    lead("s5in", c // 2 + 2, UNIT[("s5in", c // 2)] + 1)
            act.wait_ge(y_done, 16)
            tell(s.activation(gT, yT, ACT.Gelu_apprx_tanh), g_ready)
            for c in range(DC):
                wait_chunk("glu", c // 2, c % 2)
                tell(s.activation(yT[:, c, :], PB[c % 2][:, 0:T], ACT.Sigmoid), sig_done)
            ffn(1)
            ffn(2)
            lead("qkv", 0, UNIT[("qkv", 0)])
            norm(N_MOBA)
            split_h(N_MOBA)
            lead("qkv", 1, UNIT[("qkv", 0)])
            for m in range(6):
                if m < 5:
                    lead("qkv", 2 * m + 2, UNIT[("qkv", 2 * m)] + 1)
                act.wait_ge(unit_done, UNIT[("qkv", 2 * m + 1)] + 1)
                tell(s.copy(qkv[:, 0, 4 * m:4 * m + 4, :], PB[2 + 2 * (m % 2)][:, :].rearrange("p (h d) -> p h d", h=4)),
                     mq_act)
                if m < 5:
                    lead("qkv", 2 * m + 3, UNIT[("qkv", 2 * m + 1)] + 1)
            act.wait_ge(hvar_ready, 2)
            tell(s.activation(hstat[:, 1, :], hstat[:, 0, :], ACT.Sqrt), hroot_ready)
            for i in (0, 2, 4, 6):
                act.wait_ge(mqT_full, i + 1)
                dst = (mqT if i < 4 else mkT)[:, 2 * (i % 4):2 * (i % 4) + 2, :]
                tell(s.copy(dst, PB[6][:, :].rearrange("p (h q) -> p h q", h=2)), mqT_act)
            for t in range(TT):
                softmax(2, t, mL, (t + 1) * P, MD ** -0.5, mPT, 6)
            ffn(3)

        @block.gpsimd
        def _(pool):
            g = nc.gpsimd
            count = Count()

            def tell(ins, sm):
                ins.then_inc(sm, 1)
                pool.wait_ge(sm, count.up(sm))

            def link(ins):
                tell(ins, pool_link)

            link(g.memset(ident[:, :], 0.0))
            tell(g.affine_select(out=ident[:, :], in_=ident[:, :], pattern=[[-1, P]], compare_op=ALU.not_equal,
                                 fill=1.0, base=0, channel_multiplier=1), ident_ready)
            link(g.iota(iotai[:, 0:PK], pattern=[[1, PK]], base=0, channel_multiplier=0))
            tell(g.tensor_copy(iota16[:, :], iotai[:, 0:PK]), ident_ready)
            tell(g.iota(iotai[:, :], pattern=[[1, T]], base=1, channel_multiplier=0), ident_ready)
            tell(g.memset(pT[:, :, 0:16], 0.0), ident_ready)
            pool.wait_ge(tz_done, 6)
            src, dst = pT, pw0
            for st in range(4):
                d = 1 << st
                lo = 2 * d - 1
                link(g.tensor_tensor(dst[:, st:4, lo:PW], src[:, st:4, lo:PW], src[:, st:4, lo - d:PW - d], ALU.add))
                src, dst = dst, (pw1 if dst is pw0 else pw0)
            pool.wait_ge(rcnt_ready, 1)
            for w in range(4):
                sums = pw0 if w % 2 == 0 else pw1
                link(g.tensor_tensor(pw0[:, w, 0:T] if w % 2 else sums[:, w, 0:T], sums[:, w, 16:PW], rcnt[:, w, :],
                                     ALU.mult))
            tell(g.tensor_tensor(pw0[:, :, 0:T], pw0[:, :, 0:T], pT[:, :, 16:PW], ALU.subtract), mixp_ready)
            for t in range(TT):
                pool.wait_ge(route_ready, t + 1)
                with pool.Fori(0, NSLOT // UVB) as i:
                    for j in range(UVB):
                        pool.wait_ge(uv_used, i * UVB + (t * NSLOT + j + 1))
                        g.nop(nofuse=True)
                        g.tensor_copy(ibuf[:, j:j + 1], eidx[:, t, bass.ds(i * UVB + j, 1)]).then_inc(idx_copied, 1)
                        pool.wait_ge(idx_copied, i * UVB + (t * NSLOT + j + 1))
                        g.nop(nofuse=True)
                        g.indirect_dma_start(uv[j].rearrange("p a d -> p (a d)"), None, a["uv"],
                                             bass.IndirectOffsetOnAxis(ap=ibuf[:, j:j + 1], axis=0)).then_inc(uv_here[j], 16)
            pool.wait_ge(x_done, 8)
            pool.wait_ge(s5p_ready, 2)
            for b in range(2):
                ps = slice(b * NPAIR // 2, (b + 1) * NPAIR // 2)

                def lo_(plane):
                    return base[plane][:, ps, :].unsqueeze(2).broadcast_to([P, NPAIR // 2, 8, 16])

                def hi_(plane):
                    return base[plane][:, ps, :].unsqueeze(3).broadcast_to([P, NPAIR // 2, 8, 16])

                def grid(x):
                    return x.rearrange("p n (h l) -> p n h l", l=16)

                link(g.tensor_tensor(grid(et0), hi_(2), lo_(0), ALU.mult))
                link(g.tensor_tensor(grid(et1), hi_(3), lo_(1), ALU.mult))
                link(g.tensor_tensor(Ec[:, ps, :], et0, et1, ALU.subtract))
                link(g.tensor_tensor(grid(et0), hi_(3), lo_(0), ALU.mult))
                link(g.tensor_tensor(grid(et1), hi_(2), lo_(1), ALU.mult))
                link(g.tensor_tensor(Es[:, ps, :], et0, et1, ALU.add))
            pool.dma_start(cri, a["s5c"]).then_inc(c_here, 16)
            link(g.memset(CC.rearrange("p a b c -> p (a b c)"), 0.0))
            pool.wait_ge(c_here, 16)
            cre, cim = (s5p[:, b, :].unsqueeze(2).broadcast_to([P, NPAIR, SN]) for b in (8, 9))
            link(g.tensor_tensor(crt[:, 0, :, :], cri[:, 0, :, :], cre, ALU.mult))
            link(g.tensor_tensor(crt[:, 1, :, :], cri[:, 1, :, :], cim, ALU.mult))
            link(g.tensor_tensor(cp_re, crt[:, 0, :, :], crt[:, 1, :, :], ALU.subtract))
            link(g.tensor_tensor(crt[:, 0, :, :], cri[:, 0, :, :], cim, ALU.mult))
            link(g.tensor_tensor(crt[:, 1, :, :], cri[:, 1, :, :], cre, ALU.mult))
            link(g.tensor_tensor(cp_im, crt[:, 0, :, :], crt[:, 1, :, :], ALU.add))
            for b in range(2):
                pr, cs = slice(64 * b, 64 * b + 64), slice(SN * b, SN * (b + 1))
                link(g.tensor_copy(CC[pr, 0, :, cs], cp_re[pr]))
                link(g.tensor_scalar(CC[pr, 1, :, cs], cp_re[pr], -1.0, None, ALU.mult))
                tell(g.tensor_scalar(CC[pr, 2, :, cs], cp_im[pr], -1.0, None, ALU.mult), tab_ready)
            for i in range(16):
                q = i % 8
                ec, es = Ec[:, 4 * q:4 * q + 4, :], Es[:, 4 * q:4 * q + 4, :]
                pool.wait_ge(w_ready, i + 1)
                if i >= 2:
                    pool.wait_ge(y_full, i - 1)
                wr, wi = (s5w[:, W_AT[i % 2] + b, :, :] for b in range(2))
                o = [s5w[:, 4 + 4 * (i % 2) + k, :, :] for k in range(4)]
                g.tensor_tensor(o[0], wr, ec, ALU.mult)
                g.tensor_tensor(o[1], wi, es, ALU.mult)
                g.tensor_tensor(o[2], wr, es, ALU.mult)
                tell(g.tensor_tensor(o[3], wi, ec, ALU.mult), o_ready)
            pool.wait_ge(x_done, 24)
            link(g.memset(causal, 0.0))
            tell(g.affine_select(out=causal, in_=causal, pattern=[[-1, P]], compare_op=ALU.is_ge, fill=NEG, base=0,
                                 channel_multiplier=1), causal_ready)


def layouts(i):
    f = {k: np.asarray(v, np.float32) if np.asarray(v).dtype == np.float32 else np.asarray(v) for k, v in i.items()}

    def chunked(w, per):
        k, n = w.shape
        b = w.reshape(k // P, P, n // P, P).transpose(2, 1, 0, 3)
        return b.reshape(n // P // per, per, P, k // P, P).transpose(0, 2, 1, 3, 4).reshape(n // P // per, P, -1)

    def rows_of(w, per):
        k, n = w.shape
        return w.reshape(k // P // per, per, P, n).transpose(0, 2, 1, 3).reshape(k // P // per, P, -1)

    def colv(v):
        return v.reshape(-1, P).T

    w_in = f["w_in"][0]
    q, k, v, iq, ik, iw, zp, zg = np.split(w_in, [512, 576, 640, 896, 960, 964, 1476], axis=1)
    o = {}
    o["ada"] = np.concatenate([rows_of(f["w_ada"][0][:, r:r + ADW], 4) for r in range(0, 6 * D, ADW)])
    o["nat"] = rows_of(np.concatenate([q, k, ik, v, iw], 1), 4)
    o["tz"] = chunked(np.concatenate([iq, zp], 1), 2)
    o["zg"] = chunked(zg, 2)
    o["up"] = chunked(np.concatenate([f["w_up_attn"][0], f["w_up_pool"][0]], 0), 2)
    o["wo"] = rows_of(f["w_out"][0], 2)
    o["pq"] = chunked(f["w_peer_q"][0], 2)
    ff = []
    for layer in range(2):
        for b in range(2):
            g = chunked(f["ffn_w_gate_2"][layer, b], 1)
            u = chunked(f["ffn_w_up_2"][layer, b], 1)
            d = rows_of(f["ffn_w_down_2"][layer, b], 1)
            ff.append(np.concatenate([g, u, d], 2))
    o["ffn"] = np.concatenate(ff, 0)
    o["s5in"] = chunked(f["s5_w_in_2"][0], 2)
    sb_ = np.zeros((2, 8, 4, 2, SN, 4, 2, SP_), np.float32)
    for b, name in enumerate(("s5_b_re_2", "s5_b_im_2")):
        bb = f[name][0].reshape(8, 4, 2, SP_, SN)
        for j in range(4):
            for g in range(2):
                sb_[b, :, j, g, :, j, g, :] = bb[:, j, g].transpose(0, 2, 1)
    sb_ = sb_.reshape(2, 4, 2, P, 4 * P).transpose(1, 3, 2, 0, 4).reshape(4, P, -1)
    o["s5b"] = np.concatenate([sb_, sb_], 0)
    o["s5c"] = np.stack([f[n][0].reshape(NPAIR, 2, SN, SP_).transpose(1, 3, 0, 2).reshape(P, NPAIR, SN)
                         for n in ("s5_c_re_2", "s5_c_im_2")], 1)
    o["glu"] = chunked(f["s5_w_glu_2"][0], 2)
    o["s5out"] = rows_of(f["s5_w_out_2"][0], 2)
    qkv = f["moba_w_qkv_2"][0]
    o["qkv"] = np.stack([rows_of(qkv[:, 512 * m:512 * (m + 1)], 4) for m in range(6)]).reshape(12, P, -1)
    o["mo"] = rows_of(f["moba_w_out_2"][0], 2)

    def pairs(v):
        return v.reshape(NPAIR, P).T

    fn, mn = f["ffn_norm_2"], f["mix_norm_2"]
    o["cols"] = np.concatenate([
        colv(f["c"][0]), colv(f["b_ada"][0]), colv(f["g_norm1"][0]), colv(f["g_norm2"][0]),
        colv(fn[0, 0]), colv(mn[0]), colv(fn[0, 1]), colv(fn[1, 0]), colv(mn[1]), colv(fn[1, 1]),
        colv(f["s_pool"][0].reshape(-1)), colv(f["s5_d_2"][0]),
        pairs(f["s5_a_re_2"][0]), pairs(f["s5_a_im_2"][0]),
        pairs(np.broadcast_to(f["s5_log_dt_2"][0][:, None], (SG, SP_)))], 1)
    o["rows"] = np.concatenate([f["g_q"][0], f["g_k"][0], f["g_ik"][0],
                                f["moba_q_norm_2"][0], f["moba_k_norm_2"][0]])
    inv = np.float32(500000.0) ** (-np.arange(0, 2 * ROT, 2, dtype=np.float32) / np.float32(2 * ROT))
    ang = np.arange(T, dtype=np.float32)[:, None] * inv[None, :]
    o["rope"] = np.stack([np.cos(ang), np.sin(ang)], 1).astype(np.float32).reshape(TT, P, 2, ROT).transpose(1, 0, 2, 3)
    o["w_grp"] = f["w_pool_grp"][0].transpose(1, 0, 2)
    sk = f["peer_subkeys"][0]
    skd = np.zeros((2, HD, PH, 2, NKEYS), np.float32)
    for b in range(2):
        skd[b, :, :, b, :] = sk[:, b].transpose(2, 0, 1)
    o["skd"] = skd.reshape(P, PH, 2 * NKEYS)
    o["uv"] = np.concatenate([f["peer_u"][0], f["peer_v"][0]], 1)
    o["x"] = f["x"][0]
    return {n: np.ascontiguousarray(x) for n, x in o.items()}


def program(nc, arrays):
    args = {n: nc.dram_tensor(f"in_{n}", x.shape, mybir.dt.from_np(x.dtype), kind="ExternalInput").ap()
            for n, x in arrays.items()}
    out = nc.dram_tensor("out_0", (T, D), F32, kind="ExternalOutput").ap()
    build(nc, args, out)


def kernel(**inputs):
    import concourse.bacc as bacc
    from concourse.bass_utils import run_bass_kernel_spmd

    arrays = layouts(inputs)
    nc = bacc.Bacc("TRN2", target_bir_lowering=False, num_devices=1)
    program(nc, arrays)
    r = run_bass_kernel_spmd(nc, [{f"in_{n}": x for n, x in arrays.items()}], core_ids=[0])
    return r.results[0]["out_0"].reshape(1, T, D)
```
